# Optimizing a Trainium2 kernel written in Bass

```python
import math
import jax, jax.numpy as jnp
from jax import lax
import numpy as np

D_MODEL = 1024
BATCH = 1
SEQ = 256
DEPTH = 2
DEC_BATCH = 8
DEC_SEQ = 1
PAST_LEN = 2048
PAGE_SIZE = 128

D_CONV = D_MODEL
CONV_W = 3
N_HEADS = 4
D_MLSTM = 2 * D_MODEL
DV = D_MLSTM // N_HEADS
DK = DV // 2
D_QK = N_HEADS * DK
CHUNK = 64
D_FF = 2816
EPS = 1e-6
IN_SIZES = (D_CONV, D_CONV, D_CONV, D_QK, D_QK, D_MLSTM, D_MLSTM, N_HEADS, N_HEADS, D_MODEL, D_MODEL)
IN_COLS = 3 * D_CONV + 2 * D_QK + 2 * D_MLSTM + 2 * N_HEADS + 2 * D_MODEL

kernel_name = 'gated_conv_mlstm_macaron_step'

def rmsnorm(x, g):
    xf = x.astype(jnp.float32)
    y = xf * lax.rsqrt(jnp.mean(xf * xf, axis=-1, keepdims=True) + EPS)
    return (y * g.astype(jnp.float32)).astype(x.dtype)

def swiglu(x, w_gu, w_down):
    g, u = jnp.split(x @ w_gu, 2, axis=-1)
    return (jax.nn.silu(g) * u) @ w_down

def short_conv(u, buf, w):
    S = u.shape[1]
    full = jnp.concatenate([buf.astype(u.dtype), u], axis=1)
    y = full[:, 0:S] * w[0]
    for j in range(1, CONV_W):
        y = y + full[:, j:j + S] * w[j]
    return y, full[:, S:]

def _mlstm_chunk(carry, inp):
    C, n, m = carry
    qc, kc, vc, ic, fc = inp
    L = qc.shape[2]
    b = jnp.cumsum(fc, axis=-1)
    causal = jnp.tril(jnp.ones((L, L), dtype=bool))
    dlog = jnp.where(causal, b[..., :, None] - b[..., None, :] + ic[..., None, :], -jnp.inf)
    inter = b + m[..., None]
    m_row = jnp.maximum(inter, jnp.max(dlog, axis=-1))
    s = jnp.einsum('bhtk,bhsk->bhts', qc, kc) * jnp.exp(dlog - m_row[..., None])
    sc = jnp.exp(inter - m_row)
    num = sc[..., None] * jnp.einsum('bhtk,bhkv->bhtv', qc, C) + jnp.einsum('bhts,bhsv->bhtv', s, vc)
    den = sc * jnp.einsum('bhtk,bhk->bht', qc, n) + jnp.sum(s, axis=-1)
    h = num / jnp.maximum(jnp.abs(den), jnp.exp(-m_row))[..., None]
    b_last = b[..., -1]
    wlog = b_last[..., None] - b + ic
    m_new = jnp.maximum(b_last + m, jnp.max(wlog, axis=-1))
    decay = jnp.exp(b_last + m - m_new)
    wk = jnp.exp(wlog - m_new[..., None])[..., None] * kc
    C_new = decay[..., None, None] * C + jnp.einsum('bhsk,bhsv->bhkv', wk, vc)
    n_new = decay[..., None] * n + jnp.sum(wk, axis=2)
    return (C_new, n_new, m_new), h

def mlstm(q, k, v, i_pre, log_f, C0, n0, m0):
    Bn, S = q.shape[0], q.shape[1]
    L = math.gcd(S, CHUNK)
    NC = S // L
    f32 = jnp.float32
    def chunks(a):
        a = a.astype(f32).reshape((Bn, NC, L) + a.shape[2:])
        return jnp.moveaxis(jnp.moveaxis(a, 1, 0), 2, 3) if a.ndim == 5 else jnp.transpose(a, (1, 0, 3, 2))
    inp = (chunks(q * (DK ** -0.5)), chunks(k), chunks(v), chunks(i_pre), chunks(log_f))
    carry0 = (C0.astype(f32), n0.astype(f32), m0.astype(f32))
    (C, n, m), hs = lax.scan(_mlstm_chunk, carry0, inp)
    h = jnp.transpose(hs, (1, 0, 3, 2, 4)).reshape(Bn, S, N_HEADS, DV)
    return h, C.astype(C0.dtype), n.astype(n0.dtype), m.astype(m0.dtype)

def token_mixer(h, conv_buf, C0, n0, m0, w_in, w_conv, b_igate, b_fgate, g_head, w_proj_a, w_proj_b, w_out):
    Bn, S, _ = h.shape
    z = h @ w_in
    idx, acc = [], 0
    for s_ in IN_SIZES[:-1]:
        acc += s_
        idx.append(acc)
    gb, gc, xa, q, k, v, o, ip, fp, ga, gm = jnp.split(z, idx, axis=-1)
    yc, new_buf = short_conv(gc * xa, conv_buf, w_conv)
    ya = (gb * yc) @ w_proj_a
    q = q.reshape(Bn, S, N_HEADS, DK)
    k = k.reshape(Bn, S, N_HEADS, DK)
    v = v.reshape(Bn, S, N_HEADS, DV)
    i_pre = (ip + b_igate).astype(jnp.float32)
    log_f = jax.nn.log_sigmoid((fp + b_fgate).astype(jnp.float32))
    hb, C, n, m = mlstm(q, k, v, i_pre, log_f, C0, n0, m0)
    hb = hb * lax.rsqrt(jnp.mean(hb * hb, axis=-1, keepdims=True) + EPS)
    hb = (hb * g_head.reshape(N_HEADS, DV).astype(jnp.float32)).reshape(Bn, S, D_MLSTM).astype(h.dtype)
    yb = (jax.nn.sigmoid(o) * hb) @ w_proj_b
    mix = jax.nn.sigmoid(ga) * ya + jax.nn.sigmoid(gm) * yb
    return mix @ w_out, new_buf, C, n, m

def layer(x, conv_buf, C0, n0, m0, g_ffn1, w_ffn1_gu, w_ffn1_down, g_mix, w_in, w_conv, b_igate, b_fgate,
          g_head, w_proj_a, w_proj_b, w_out, g_ffn2, w_ffn2_gu, w_ffn2_down):
    x = x + 0.5 * swiglu(rmsnorm(x, g_ffn1), w_ffn1_gu, w_ffn1_down)
    y, nb, C, n, m = token_mixer(rmsnorm(x, g_mix), conv_buf, C0, n0, m0, w_in, w_conv, b_igate, b_fgate,
                                 g_head, w_proj_a, w_proj_b, w_out)
    x = x + y
    x = x + 0.5 * swiglu(rmsnorm(x, g_ffn2), w_ffn2_gu, w_ffn2_down)
    return x, nb, C, n, m

def setup_inputs(seed: int = 0) -> dict:
    key = jax.random.key(seed)
    ks = jax.random.split(key, 24)
    nrm = lambda k, shp, s: jax.random.normal(k, shp, jnp.float32) * s
    gain = lambda k, shp: 1.0 + 0.05 * jax.random.normal(k, shp, jnp.float32)
    return {
        'x_prompt': nrm(ks[0], (BATCH, SEQ, D_MODEL), 1.0),
        'x_sample': nrm(ks[1], (DEC_BATCH, DEC_SEQ, D_MODEL), 1.0),
        'state_conv': nrm(ks[2], (DEPTH, DEC_BATCH, CONV_W - 1, D_CONV), 1.0),
        'state_mlstm_c': nrm(ks[3], (DEPTH, DEC_BATCH, N_HEADS, DK, DV), 1.0),
        'state_mlstm_n': nrm(ks[4], (DEPTH, DEC_BATCH, N_HEADS, DK), 1.0),
        'state_mlstm_m': nrm(ks[5], (DEPTH, DEC_BATCH, N_HEADS), 1.0),
        'g_ffn1': gain(ks[6], (DEPTH, D_MODEL)),
        'w_ffn1_gu': nrm(ks[7], (DEPTH, D_MODEL, 2 * D_FF), D_MODEL ** -0.5),
        'w_ffn1_down': nrm(ks[8], (DEPTH, D_FF, D_MODEL), D_FF ** -0.5),
        'g_mix': gain(ks[9], (DEPTH, D_MODEL)),
        'w_in': nrm(ks[10], (DEPTH, D_MODEL, IN_COLS), D_MODEL ** -0.5),
        'w_conv': nrm(ks[11], (DEPTH, CONV_W, D_CONV), CONV_W ** -0.5),
        'b_igate': nrm(ks[12], (DEPTH, N_HEADS), 0.1),
        'b_fgate': jnp.linspace(3.0, 6.0, N_HEADS, dtype=jnp.float32) + nrm(ks[13], (DEPTH, N_HEADS), 0.1),
        'g_head': gain(ks[14], (DEPTH, D_MLSTM)),
        'w_proj_a': nrm(ks[15], (DEPTH, D_CONV, D_MODEL), D_CONV ** -0.5),
        'w_proj_b': nrm(ks[16], (DEPTH, D_MLSTM, D_MODEL), D_MLSTM ** -0.5),
        'w_out': nrm(ks[17], (DEPTH, D_MODEL, D_MODEL), D_MODEL ** -0.5),
        'g_ffn2': gain(ks[18], (DEPTH, D_MODEL)),
        'w_ffn2_gu': nrm(ks[19], (DEPTH, D_MODEL, 2 * D_FF), D_MODEL ** -0.5),
        'w_ffn2_down': nrm(ks[20], (DEPTH, D_FF, D_MODEL), D_FF ** -0.5),
        'g_final': gain(ks[21], (D_MODEL,)),
    }

def reference(x_prompt, x_sample, state_conv, state_mlstm_c, state_mlstm_n, state_mlstm_m,
              g_ffn1, w_ffn1_gu, w_ffn1_down, g_mix, w_in, w_conv, b_igate, b_fgate, g_head,
              w_proj_a, w_proj_b, w_out, g_ffn2, w_ffn2_gu, w_ffn2_down, g_final):
    bp = x_prompt.shape[0]
    dt = x_prompt.dtype
    xp, xs = x_prompt, x_sample
    conv_p, c_p, n_p, m_p = [], [], [], []
    conv_s, c_s, n_s, m_s = [], [], [], []
    for l in range(DEPTH):
        w = (g_ffn1[l], w_ffn1_gu[l], w_ffn1_down[l], g_mix[l], w_in[l], w_conv[l], b_igate[l], b_fgate[l],
             g_head[l], w_proj_a[l], w_proj_b[l], w_out[l], g_ffn2[l], w_ffn2_gu[l], w_ffn2_down[l])
        xp, nb, C, n, m = layer(xp, jnp.zeros((bp, CONV_W - 1, D_CONV), dt),
                                jnp.zeros((bp, N_HEADS, DK, DV), dt), jnp.zeros((bp, N_HEADS, DK), dt),
                                jnp.zeros((bp, N_HEADS), dt), *w)
        conv_p.append(nb); c_p.append(C); n_p.append(n); m_p.append(m)
        xs, nb, C, n, m = layer(xs, state_conv[l], state_mlstm_c[l], state_mlstm_n[l], state_mlstm_m[l], *w)
        conv_s.append(nb); c_s.append(C); n_s.append(n); m_s.append(m)
    y_prompt = rmsnorm(xp, g_final)
    y_sample = rmsnorm(xs, g_final)
    return (y_prompt, y_sample,
            jnp.stack(conv_p), jnp.stack(c_p), jnp.stack(n_p), jnp.stack(m_p),
            jnp.stack(conv_s), jnp.stack(c_s), jnp.stack(n_s), jnp.stack(m_s))


_drawn_inputs = setup_inputs


def setup_inputs(seed=0):
    import zlib

    import numpy as np

    out = dict(_drawn_inputs(seed))
    spreads = {}
    factors = {'g_head': 2.923}
    for name, (base, spread) in spreads.items():
        noise = np.random.default_rng([zlib.crc32(name.encode()), seed]).standard_normal(out[name].shape)
        drawn = base * np.exp(spread * noise) if base else spread * noise
        out[name] = __import__('jax').numpy.asarray(drawn.astype(out[name].dtype))
    for name, factor in factors.items():
        out[name] = (out[name] * factor).astype(out[name].dtype)
    return out
```

```python
import concourse.bass as bass
from concourse import mybir
from contextlib import ExitStack

F32 = mybir.dt.float32
F32R = mybir.dt.float32r
ACT = mybir.ActivationFunctionType
ALU = mybir.AluOpType

P = 128
DEPTH = 2
D = 1024
NP, NS = 256, 8
T = NP + NS
H, DK, DV = 4, 256, 512
D_FF = 2816
EPS = 1e-6
KT = D // P
FT = D_FF // P
VT_TILES = H * DV // P
VPH = DV // P
KPH = DK // P
GATE_COL = 3 * D + 2 * H * DK + 2 * H * DV
SLOTS = 4
CK = 4
GW = 2 * P
CHUNK = CK * GW

FFN_PAIRS = D_FF // GW
DOWN_CHUNKS = -(-FT // CK)
DOWN_GROUPS = D // GW
C_DOWN = FFN_PAIRS * 4
FFN_CHUNKS = C_DOWN + DOWN_CHUNKS * DOWN_GROUPS
FFN_GROUPS = 2 * FFN_PAIRS + DOWN_GROUPS
UNIT_GROUPS = D // GW
C_IN = FFN_CHUNKS
C_PA = C_IN + 11 * UNIT_GROUPS * 2
C_PB = C_PA + 4 * 2
C_WO = C_PB + 4 * 4
C_FFN2 = C_WO + 4 * 2
CHUNKS = C_FFN2 + FFN_CHUNKS
G_IN = FFN_GROUPS
G_PA = G_IN + 11 * UNIT_GROUPS
G_PB = G_PA + 4
G_WO = G_PB + 4
G_FFN2 = G_WO + 4
GROUPS = G_FFN2 + FFN_GROUPS
assert CHUNKS % SLOTS == 0 and C_IN % SLOTS == 0 and GROUPS % 2 == 0 and G_IN % 2 == 0
SCRATCH = 2048
AHEAD = 3

U_GB, U_GC, U_XA, U_Q, U_K, U_V, U_O = 0, 1, 2, 3, 4, 5, 7
ORDER_G = {name: G_IN + UNIT_GROUPS * n for n, name in enumerate(["q", "k", "v0", "v1", "gc", "xa", "gb", "o0", "o1", "ga", "gm"])}

PAR_FFN1, PAR_MIX, PAR_FFN2, PAR_CONV, PAR_HEAD, PARS = 0, 8, 16, 24, 48, 64
OP_NORM1, OP_NORM2, OP_YA, OP_MIX, OP_NORM3, OPS = 0, 8, 16, 24, 32, 40
SM_AW, SM_S, SM_N, SM_CV, SM_END = 0, 24, 120, 184, 312
NORMS = 3


def build_program(nc, x_prompt, x_sample, state_conv, state_c, state_n, state_m, g_ffn1, w_gu1, w_dn1,
                  g_mix, w_in, w_conv, b_i, b_f, g_head, w_pa, w_pb, w_out, g_ffn2, w_gu2, w_dn2, g_final,
                  y_prompt, y_sample, conv_p, c_p, n_p, m_p, conv_s, c_s, n_s, m_s):
    with ExitStack() as ctx:
        def sb(name, shape, dt=F32):
            return ctx.enter_context(nc.sbuf_tensor(name, shape, dt))

        def sem(name):
            return ctx.enter_context(nc.semaphore(name))

        X = sb("residual", [P, KT, T])
        A_h = sb("operand_hi", [P, KT, T], F32R)
        A_l = sb("operand_lo", [P, KT, T], F32R)
        wide = sb("wide_operand", [P, 2 * FT, T], F32R)
        G_h, G_l = wide[:, 0:FT, :], wide[:, FT:2 * FT, :]
        B_h, B_l = wide[:, 0:VT_TILES, :], wide[:, VT_TILES:2 * VT_TILES, :]
        v_rows = wide[:, 2 * VT_TILES:2 * VT_TILES + 8, :].rearrange("p a t -> p (a t)")[:, 0:H * DV]
        QK = sb("q_k", [P, 2 * KT, T])
        GA, GM = QK[:, 0:KT, :], QK[:, KT:2 * KT, :]
        VH = sb("v_heads", [P, VT_TILES, T])
        k_tok = sb("k_tokens", [P, 2, H * DK])
        v_tok = sb("v_tokens", [P, 2, H * DV])
        U = sb("conv_input", [P, KT, T])
        C = [sb(f"c_state{i}", [P, KPH, DV]) for i in range(2)] + \
            [v_tok[:, i // 2, (i % 2) * KPH * DV:(i % 2 + 1) * KPH * DV].rearrange("p (a b) -> p a b", a=KPH) for i in range(4)]
        raw = [sb(f"raw_ring{i}", [P, CHUNK]) for i in range(SLOTS)]
        hi = [sb(f"hi_ring{i}", [P, CHUNK], F32R) for i in range(SLOTS)]
        lo = [sb(f"lo_ring{i}", [P, CHUNK], F32R) for i in range(SLOTS)]
        act_tmp = sb("act_tmp", [P, 2, T])
        val = sb("value_tmp", [P, 2, T])
        val2 = sb("value_tmp2", [P, 2, T])
        sq = sb("squares", [P, 2, T])
        sq_sum = sb("square_sums", [P, 2, T])
        rstd = sb("rstd", [P, T])
        stage = sb("stage", [P, 2, DV])
        ident = sb("identity", [P, P])
        ones = sb("ones", [P, P])
        causal = sb("causal_limit", [P, NP])
        eps = sb("eps", [P, 1])
        pick = sb("pick_sample", [P, NS], F32R)
        par = sb("parameters", [P, DEPTH * PARS + KT])
        bias_i = sb("bias_i", [H, DEPTH])
        bias_f = sb("bias_f", [H, DEPTH])
        wg = sb("gate_weights", [P, KT, 2 * H])
        wg_h = sb("gate_weights_hi", [P, KT * 36 + P - 36], F32R)
        wg_l = sb("gate_weights_lo", [P, KT * 36 + P - 36], F32R)
        rows = sb("head_rows", [H, 2, NP])
        s_rows = sb("sample_rows", [H, 3, NS])
        m_new = sb("m_new", [H, NS])
        m_old = sb("m_old", [H, NS])
        n_old = sb("n_old", [NS * H, DK])
        small = sb("small_transposed", [P, SM_END])
        q_s = sb("q_samples", [P, H, KPH, NS])
        wk_s = sb("wk_samples", [P, H, KPH, NS])
        n_new = sb("n_new", [P, KPH, H, NS])
        qn = sb("q_times_n", [P, KPH, H, NS])
        qn_sum = sb("q_n_sum", [P, H, NS])
        r_den = sb("sample_reciprocal", [P, H, NS])
        gate_s = sb("sample_gate", [P, VT_TILES, NS])
        h_sum = sb("sample_square_sum", [P, H, NS])
        u_keep = sb("conv_tail", [P, KT, 2 + NS])
        np_col = sb("n_prompt_columns", [P, H * KPH])
        head_den = sb("head_denominators", [P, 2, H])
        head_ms = sb("head_square_columns", [P, 2, H])
        head_f = sb("head_factors", [P, 2, H])

        decay = sq[:, :, :].rearrange("p a t -> p (a t)")[:, 0:NP + P]
        score = val2[:, :, :].rearrange("p a t -> p (a t)")[:, 0:NP + P]
        diag = [t[:, :, :].rearrange("p a t -> p (a t)")[:, 0:4 * P].rearrange("p (s t) -> p s t", s=4) for t in (sq_sum, sq)]
        n_out = act_tmp[0:NS * H, 0, 0:DK]
        np_row = act_tmp[0:H * KPH, 1, 0:P]
        h_s = val2[:, 0, 0:P].rearrange("p (h v b) -> p h v b", h=H, v=VPH)
        h_sq = val2[:, 1, 0:P].rearrange("p (h v b) -> p h v b", h=H, v=VPH)
        gate_f = U[0:H, 0, :]
        gate_mn = U[0:H, 1, :]
        gate_na = U[0:H, 2, :]
        gate_ex = U[0:H, 3, :]
        gate_ln = U[0:H, 4, :]
        gate_lf = U[0:H, 5, :]
        gate_b = U[0:H, 6, 0:NP]
        gate_mx = U[0:H, 7, 0:NP]
        gate_i = sq[0:H, 0, :]
        s_inter = sq[0:H, 1, 0:NS]
        conv_rows = VH[0:2 * NS, 0:4, :].rearrange("p a t -> p (a t)")[:, 0:D]
        aw = VH[0:H, 12:15, 0:NP]
        aw_t = small[:, SM_AW:SM_S].rearrange("p (kind st h) -> p kind st h", kind=3, st=2)
        s_bc = small[:, SM_S:SM_N].rearrange("p (h kind b) -> p h kind b", h=H, kind=3)
        n_t = small[:, SM_N:SM_CV].rearrange("p (kt b h) -> p kt b h", kt=KPH, b=NS)
        cv_t = small[:, SM_CV:SM_END].rearrange("p (t b j) -> p t b j", t=KT, b=NS)
        x_rows = VH[:, 0:8, :].rearrange("p a t -> p (a t)")[:, 0:2 * D].rearrange("p (s d) -> p s d", s=2)
        xs_rows = VH[0:NS, 8:12, :].rearrange("p a t -> p (a t)")[:, 0:D]
        par_rows = k_tok[:, 0, 0:P]
        gf_rows = k_tok[0:KT, 1, 0:P]
        y_rows = VH[:, 0:12, :].rearrange("p a t -> p (a t)")[:, 0:3 * D].rearrange("p (s d) -> p s d", s=3)

        ps = ctx.enter_context(nc.psum_tensor("psum", [P, 8, 512], F32))
        pair = [ps[:, 0:2, 0:T], ps[:, 2:4, 0:T]]
        V_BANK, S_BANK, T_BANK = 4, 5, 6
        num_s = ps[:, S_BANK, 0:P].rearrange("p (h v b) -> p h v b", h=H, v=VPH)
        den_s = ps[:, S_BANK, P:P + H * NS]
        n_rows_ps = ps[0:NS * H, S_BANK, 256:512]
        den_c = ps[:, S_BANK, 160:168].rearrange("p (st h) -> p st h", st=2)
        ms_c = ps[:, S_BANK, 168:176].rearrange("p (st h) -> p st h", st=2)
        np_ps = ps[:, T_BANK + 1, 0:H * KPH]
        npt_ps = ps[0:H * KPH, V_BANK, 0:P]

        w_loaded = [sem(f"w_loaded{i}") for i in range(SLOTS)]
        split_hi = sem("split_hi")
        split_lo = sem("split_lo")
        chunk_done = sem("chunk_done")
        pair_free = [sem("pair0_free"), sem("pair1_free")]
        const_ready = sem("const_ready")
        passed = sem("passed")
        prep_loaded = sem("prep_loaded")
        prep_tr = sem("prep_transposed")
        prep_copied = sem("prep_copied")
        small_loaded = sem("small_loaded")
        sq_ready = sem("sq_ready")
        sums_ready = sem("sums_ready")
        norm_sum = sem("norm_sum")
        norm_root = sem("norm_root")
        operand_val = sem("operand_val")
        operand_hi = sem("operand_hi_ready")
        operand_ready = sem("operand_ready")
        hidden_hi = sem("hidden_hi")
        hidden_ready = sem("hidden_ready")
        wg_hi = sem("wg_hi")
        wg_ready = sem("wg_ready")
        gates_done = sem("gates_done")
        gate_exp_in = sem("gate_exp_in")
        gate_log = sem("gate_log")
        gate_rows = sem("gate_rows")
        gate_exps = sem("gate_exps")
        small_done = sem("small_done")
        small_copied = sem("small_copied")
        tr_done = sem("tokens_transposed")
        tr_free = [sem("tr_bank0_free"), sem("tr_bank1_free")]
        v_zero = sem("v_rows_zero")
        v_hi = sem("v_rows_hi")
        qn_ready = sem("qn_ready")
        den_done = sem("sample_den_done")
        n_out_ready = sem("n_out_ready")
        score_done = sem("score_done")
        decay_arg = sem("decay_arg")
        decay_ready = sem("decay_ready")
        score_ready = sem("score_ready")
        av_done = sem("av_done")
        av_read = sem("av_read")
        columns_done = sem("columns_done")
        columns_read = sem("columns_read")
        head_root = sem("head_root")
        diag_ready = sem("diag_ready")
        factors_done = sem("factors_done")
        cp_done = sem("c_prompt_done")
        cp_copied = sem("c_prompt_copied")
        np_done = sem("n_prompt_done")
        np_copied = sem("n_prompt_copied")
        npt_done = sem("n_prompt_transposed")
        npt_copied = sem("n_prompt_rows_copied")
        tail_done = sem("tail_transposed")
        tail_copied = sem("tail_copied")
        c_loaded = [sem(f"c_loaded{i}") for i in range(6)]
        c_stored = [sem(f"c_stored{i}") for i in range(6)]
        vbc_done = sem("value_broadcast")
        c_scaled = sem("c_scaled")
        c_new = sem("c_new")
        num_done = sem("sample_num_done")
        hs_sum_ready = sem("sample_sum_ready")
        hs_sum = sem("sample_sum_done")
        hs_root = sem("sample_root")
        b_ready = sem("gated_heads_ready")
        y_tiles = sem("y_tiles")
        y_tr = sem("y_transposed")
        y_copied = sem("y_copied")
        stored = sem("stored")
        m_stored = sem("m_stored")
        stage_stored = [sem("stage_stored0"), sem("stage_stored1")]
        n_stored = sem("n_stored")
        PER_SLOT = [8, 8, 4, 4, 4, 4]
        SMALL_LOADS = 5
        STAGE_STORES = H + 1
        PREP_LOADS = 3 + DEPTH * 5 + 3

        block = ctx.enter_context(nc.Block())

        def own_step(eng):
            eng.sem_inc(passed, 1)

        @block.sync
        def _(sp):
            def load(l, c, slot, dst, src):
                sp.wait_ge(split_lo, l * CHUNKS + c + 1)
                own_step(sp)
                sp.dma_start(dst, src).then_inc(w_loaded[slot], 16)

            def rows_of(w, l, k0, n, col):
                return w[bass.ds(l, 1), k0 * P:(k0 + n) * P, bass.ds(col, GW)].rearrange(
                    "a (k p) n -> p (a k) n", p=P)

            def to(slot, n=CK):
                return raw[slot][:, 0:n * GW].rearrange("p (k n) -> p k n", n=GW)

            def ffn(l, base, w_gu, w_dn):
                with sp.Fori(0, FFN_PAIRS) as i:
                    for j in range(4):
                        load(l, i * 4 + (base + j), j, to(j),
                             rows_of(w_gu, l, CK * (j % 2), CK, i * GW + (j // 2) * D_FF))
                with sp.Fori(0, DOWN_GROUPS // 2) as i:
                    for j in range(2 * DOWN_CHUNKS):
                        k0 = CK * (j % DOWN_CHUNKS)
                        n = min(CK, FT - k0)
                        load(l, i * (2 * DOWN_CHUNKS) + (base + C_DOWN + j), j % SLOTS, to(j % SLOTS, n),
                             rows_of(w_dn, l, k0, n, i * (2 * GW) + GW * (j // DOWN_CHUNKS)))

            def unit(l, c0, col):
                for j in range(8):
                    load(l, c0 + j, j % SLOTS, to(j % SLOTS), rows_of(w_in, l, CK * (j % 2), CK, col + GW * (j // 2)))

            with sp.Fori(0, DEPTH) as l:
                ffn(l, 0, w_gu1, w_dn1)
                with sp.Fori(0, 4) as i:
                    unit(l, i * 8 + C_IN, i * D + U_Q * D)
                unit(l, C_IN + 32, U_GC * D)
                unit(l, C_IN + 40, U_XA * D)
                unit(l, C_IN + 48, U_GB * D)
                with sp.Fori(0, 2) as i:
                    unit(l, i * 8 + (C_IN + 56), i * D + U_O * D)
                with sp.Fori(0, 2) as i:
                    unit(l, i * 8 + (C_IN + 72), i * D + (GATE_COL + 2 * H))
                with sp.Fori(0, 2) as i:
                    for j in range(4):
                        load(l, i * 4 + (C_PA + j), j, to(j), rows_of(w_pa, l, CK * (j % 2), CK, i * (2 * GW) + GW * (j // 2)))
                with sp.Fori(0, 4) as i:
                    for j in range(4):
                        load(l, i * 4 + (C_PB + j), j, to(j), rows_of(w_pb, l, CK * j, CK, i * GW))
                with sp.Fori(0, 2) as i:
                    for j in range(4):
                        load(l, i * 4 + (C_WO + j), j, to(j), rows_of(w_out, l, CK * (j % 2), CK, i * (2 * GW) + GW * (j // 2)))
                ffn(l, C_FFN2, w_gu2, w_dn2)

        @block.gpsimd
        def _(pool):
            pool.memset(ident[:, :], 0.0)
            pool.memset(causal[:, :], 0.0)
            pool.memset(eps[:, :], EPS)
            pool.drain()
            pool.affine_select(out=ident[:, :], in_=ident[:, :], compare_op=ALU.not_equal, fill=1.0, base=0,
                               pattern=[[-1, P]], channel_multiplier=1)
            pool.affine_select(out=causal[:, :], in_=causal[:, :], compare_op=ALU.is_ge, fill=-1e30, base=0,
                               pattern=[[1, NP]], channel_multiplier=-1)
            pool.memset(wg_h[:, :].bitcast(F32), 0.0)
            pool.memset(wg_l[:, :].bitcast(F32), 0.0).then_inc(const_ready, 1)

            for s in (chunk_done, *pair_free, *tr_free, *c_stored, *stage_stored, n_stored, m_stored, c_new, b_ready):
                pool.sem_inc(s, 1)

            with pool.Fori(0, DEPTH) as l:
                pool.wait_ge(chunk_done, 1 + l * CHUNKS + C_IN)
                own_step(pool)
                pool.memset(v_rows[:, :].bitcast(F32), 0.0).then_inc(v_zero, 1)

                def load_c(n, s, stores, b, h):
                    pool.wait_ge(num_done, l * (NS * H) + (n + (1 if s < 2 else -1)))
                    pool.wait_ge(c_stored[s], 1 + l * (16 * PER_SLOT[s]) + stores * 16)
                    pool.dma_start(C[s][:, :, :], state_c[bass.ds(l, 1), b, bass.ds(h, 1)].rearrange(
                        "x y (kt p) v -> p (x y kt) v", p=P)).then_inc(c_loaded[s], 16)

                for n in range(12):
                    load_c(n, n % 2, n // 2, 4 + n // H, n % H)
                pool.wait_ge(cp_copied, l * (2 * H) + 2 * H)
                own_step(pool)
                with pool.Fori(0, H) as h:
                    for b in range(4):
                        load_c(h * 4 + (12 + b), 2 + b, h, b, h)
                with pool.Fori(0, 2) as i:
                    for x in range(2):
                        load_c(i * 2 + (28 + x), x, i + 6, NS - 1, i * 2 + x)

        def act_split(act, l, c, slot):
            act.wait_ge(w_loaded[slot], l * (16 * CHUNKS // SLOTS) + (c - slot) * 4 + 16)
            act.activation(hi[slot][:, :], raw[slot][:, :], ACT.Copy).then_inc(split_hi, 1)

        def dve_split(dve, l, c, slot):
            dve.wait_ge(split_hi, l * CHUNKS + c + 1)
            dve.tensor_tensor(lo[slot][:, :], raw[slot][:, :], hi[slot][:, :].bitcast(F32),
                              ALU.subtract).then_inc(split_lo, 1)

        def token_dst(t):
            n, dst = (t, k_tok) if t < 4 else (t - 4, v_tok)
            return dst[:, n % 2, (n // 2) * 512:(n // 2 + 1) * 512]

        def l1_states(i, j):
            if i < 4:
                return ()
            return (i - 4,) if i < 8 and j == 0 else (4 + 2 * (i - 8) + j,) if i >= 8 else ()

        @block.scalar
        def _(act):
            def ahead(l, c, j):
                act.wait_ge(chunk_done, 1 + l * CHUNKS + c)
                act_split(act, l, c + AHEAD, (j + AHEAD) % SLOTS)

            def wait_group(l, c_end):
                act.wait_ge(chunk_done, 1 + l * CHUNKS + c_end)

            for s in range(2):
                act.dma_start(x_rows[:, s, :], x_prompt[0, s * P:(s + 1) * P, :]).then_inc(prep_loaded, 16)
            act.dma_start(xs_rows, x_sample[:, 0, :]).then_inc(prep_loaded, 16)
            for i in range(DEPTH):
                for off, n, src in ((PAR_FFN1, 8, g_ffn1[i]), (PAR_MIX, 8, g_mix[i]), (PAR_FFN2, 8, g_ffn2[i]),
                                    (PAR_CONV, 24, w_conv[i].rearrange("j d -> (j d)")), (PAR_HEAD, 16, g_head[i])):
                    at = i * PARS + off
                    act.dma_start(par_rows[at:at + n, :], src.rearrange("(t p) -> t p", p=P)).then_inc(prep_loaded, 16)
            act.dma_start(gf_rows, g_final.rearrange("(t p) -> t p", p=P)).then_inc(prep_loaded, 16)
            act.dma_start(bias_i[:, :], b_i.rearrange("l h -> h l"), allow_slow_non_contiguous=True).then_inc(prep_loaded, 16)
            act.dma_start(bias_f[:, :], b_f.rearrange("l h -> h l"), allow_slow_non_contiguous=True).then_inc(prep_loaded, 16)

            norm_n = [0]

            def squares(l, q, g=None):
                n = norm_n[0]
                norm_n[0] += 1
                if g is None:
                    act.wait_ge(prep_copied, 4)
                else:
                    act.wait_ge(pair_free[g % 2], 1 + l * (GROUPS // 2) + (g // 2 + 1))
                if q >= 2:
                    act.wait_ge(sums_ready, l * (3 * NORMS) + (n // 4 * 3 + q - 1))
                dst = sq if q else sq_sum
                act.activation(dst[:, :, :], X[:, 2 * q:2 * q + 2, :], ACT.Square).then_inc(sq_ready, 1)

            def norm_root_of(l, n, scale=1.0 / D):
                act.wait_ge(norm_sum, l * NORMS + (n + 1))
                act.activation(rstd[:, :], ps[:, 7, 0:T], ACT.Sqrt, bias=eps[:, 0:1], scale=scale).then_inc(norm_root, 1)

            def norm_hi(l, n):
                for q in range(4):
                    act.wait_ge(operand_val, l * (4 * NORMS) + (4 * n + q + 1))
                    act.activation(A_h[:, 2 * q:2 * q + 2, :], (val, val2)[q % 2][:, :, :], ACT.Copy).then_inc(operand_hi, 1)

            def ffn(l, which, c0, g0):
                with act.Fori(0, FFN_PAIRS) as i:
                    for j in range(4):
                        ahead(l, i * 4 + (c0 + j), j)
                        if j == 1:
                            wait_group(l, i * 4 + (c0 + 2))
                            act.activation(act_tmp[:, :, :], pair[0], ACT.Silu).then_inc(pair_free[0], 1)
                    act.wait_ge(pair_free[1], 1 + l * (GROUPS // 2) + (i + (g0 // 2 + 1)))
                    act.activation(G_h[:, bass.ds(i * 2, 2), :], val[:, :, :], ACT.Copy).then_inc(hidden_hi, 1)
                for g in range(DOWN_GROUPS):
                    for j in range(DOWN_CHUNKS):
                        c = c0 + C_DOWN + g * DOWN_CHUNKS + j
                        if c + AHEAD < CHUNKS:
                            ahead(l, c, c)
                    squares(l, g, g0 + 2 * FFN_PAIRS + g)

            act.wait_ge(const_ready, 1)
            for q in range(4):
                squares(0, q)
            norm_n[0] = 0

            with act.Fori(0, DEPTH) as l:
                def l1(c=0):
                    return l + (1 + c)

                act.wait_ge(chunk_done, 1 + l * CHUNKS)
                act.dma_start(n_old[:, :], state_n[bass.ds(l, 1)].rearrange("a b h k -> (a b h) k")).then_inc(small_loaded, 16)
                act.dma_start(m_old[:, :], state_m[bass.ds(l, 1)].rearrange("a b h -> h (a b)"), allow_slow_non_contiguous=True).then_inc(small_loaded, 16)
                act.wait_ge(prep_tr, 4)
                act.dma_start(conv_rows, state_conv[bass.ds(l, 1)].rearrange("a b j d -> (a b j) d")).then_inc(small_loaded, 16)
                act.dma_start(wg[:, :, :], w_in[bass.ds(l, 1), :, GATE_COL:GATE_COL + 2 * H].rearrange(
                    "a (k p) n -> p (a k) n", p=P)).then_inc(small_loaded, 16)
                act.dma_start(conv_s[bass.ds(l, 1), :, 0, :], state_conv[bass.ds(l, 1), :, 1, :]).then_inc(small_loaded, 16)

                for c in range(AHEAD):
                    act_split(act, l, c, c)
                norm_root_of(l, 0)
                norm_hi(l, 0)
                norm_n[0] = 4
                ffn(l, 0, 0, 0)

                act.wait_ge(small_loaded, l * (16 * SMALL_LOADS) + 16 * SMALL_LOADS)
                for part, w0 in enumerate((0, 32)):
                    ins = act.activation(wg_h[:, 0:KT * 36].rearrange("p (k c) -> p k c", c=36)[:, :, w0:w0 + H],
                                         wg[:, :, part * H:part * H + H], ACT.Copy)
                ins.then_inc(wg_hi, 1)
                norm_root_of(l, 1)
                norm_hi(l, 1)
                act.wait_ge(gate_exp_in, l1())
                act.activation(gate_ex, gate_na, ACT.Exp)
                act.drain()
                act.activation(gate_ln, gate_ex, ACT.Ln, bias=ones[0:H, 0:1]).then_inc(gate_log, 1)
                act.wait_ge(gate_rows, l1())
                act.activation(aw[:, 1, :], aw[:, 0, :], ACT.Exp, bias=rows[:, 0, NP - 1:NP])
                act.activation(aw[:, 2, :], rows[:, 1, :], ACT.Exp, scale=-1.0)
                act.activation(s_rows[:, :, :], s_rows[:, :, :], ACT.Exp).then_inc(gate_exps, 1)
                act.dma_start(m_p[bass.ds(l, 1), 0, :].rearrange("a h -> h a"), rows[:, 1, NP - 1:NP], allow_slow_non_contiguous=True).then_inc(m_stored, 16)
                act.dma_start(m_s[bass.ds(l, 1)].rearrange("a b h -> h (a b)"), m_new[:, :], allow_slow_non_contiguous=True).then_inc(m_stored, 16)

                def unit(c0, evac, sample=lambda g, s: None, last=lambda g: None):
                    for g in range(4):
                        for j in range(2):
                            sample(g, j)
                            ahead(l, c0 + 2 * g + j, 2 * g + j)
                        wait_group(l, c0 + 2 * g + 2)
                        evac(g)
                        last(g)

                with act.Fori(0, 2) as i:
                    unit(i * 8 + C_IN, lambda g: act.activation(
                        QK[:, bass.ds(i * 8 + 2 * g, 2), :], pair[g % 2], ACT.Copy).then_inc(pair_free[g % 2], 1))
                act.wait_ge(small_copied, l1())
                with act.Fori(0, 2) as i:
                    unit(i * 8 + (C_IN + 16), lambda g: act.activation(
                        VH[:, bass.ds(i * 8 + 2 * g, 2), :], pair[g % 2], ACT.Copy).then_inc(pair_free[g % 2], 1))

                def scale_c(n, s, stores, b, h):
                    act.wait_ge(c_loaded[s], l * (16 * PER_SLOT[s]) + (stores * 16 + 16))
                    act.activation(C[s][:, :, :], C[s][:, :, :], ACT.Copy,
                                   scale=s_bc[:, bass.ds(h, 1), 0, b:b + 1].rearrange("p a c -> p (a c)")).then_inc(c_scaled, 1)

                def store_c(n, s, b, h):
                    act.wait_ge(c_new, 1 + l * (NS * H) + (n + 1))
                    act.dma_start(c_s[bass.ds(l, 1), b, bass.ds(h, 1)].rearrange("x y (kt p) v -> p (x y kt) v", p=P),
                                  C[s][:, :, :]).then_inc(c_stored[s], 16)

                def samples(i, n0):
                    h = i + (n0 - 12) // 4
                    def step(g, j):
                        if j == 0:
                            scale_c(i * 4 + (n0 + g), 2 + g, h, g, h)
                    return step, lambda g: store_c(i * 4 + (n0 + g), 2 + g, g, h)

                def token_copy(t):
                    act.wait_ge(tr_done, l * 16 + (t + 1))
                    act.activation(token_dst(t), ps[:, T_BANK + t % 2, :], ACT.Copy).then_inc(tr_free[t % 2], 1)

                def v_row_hi(t):
                    act.wait_ge(v_zero, l1())
                    act.wait_ge(tr_done, l * 16 + (t + 1))
                    act.activation(v_rows[0:NS, (t - 12) * 512:(t - 11) * 512], ps[0:NS, T_BANK + t % 2, :],
                                   ACT.Copy).then_inc(v_hi, 1)

                def head_exps(h):
                    act.wait_ge(decay_arg, l * H + (h + 1))
                    act.activation(decay, decay, ACT.Exp).then_inc(decay_ready, 1)

                def head_square(h):
                    act.wait_ge(av_done, l * H + (h + 1))
                    both = ps[:, T_BANK:T_BANK + 2, :].rearrange("p a (b t) -> p (a b) t", b=2)
                    if h == 0:
                        for s in range(2):
                            act.wait_ge(stage_stored[s], 1 + l * (16 * STAGE_STORES))
                    else:
                        act.wait_ge(columns_done, l * H + h)
                    act.activation(stage[:, :, :].rearrange("p a (b t) -> p (a b) t", b=2), both, ACT.Square)
                    act.activation(VH[:, VPH * h:VPH * h + VPH, 0:NP], both, ACT.Copy).then_inc(av_read, 1)

                def l1_state(i, j):
                    for n in l1_states(i, j):
                        scale_c(n, n % 2, n // 2, 4 + n // H, n % H)

                def l1_last(i):
                    for j in range(2):
                        for n in l1_states(i, j):
                            store_c(n, n % 2, 4 + n // H, n % H)
                    if i < 3:
                        for t in range(4 * i, 4 * i + 4):
                            token_copy(t)
                    if i == 3:
                        for t in range(12, 16):
                            v_row_hi(t)
                    if i >= 3 and i % 2 == 1 and i < 11:
                        head_exps((i - 3) // 2)
                    if i >= 4 and i % 2 == 0:
                        head_square((i - 4) // 2)

                def nothing(g):
                    pass

                unit(C_IN + 32, lambda g: act.activation(U[:, 2 * g:2 * g + 2, :], pair[g % 2], ACT.Copy)
                     .then_inc(pair_free[g % 2], 1), last=l1_last)
                unit(C_IN + 40, nothing, lambda g, j: l1_state(4 + g, j), lambda g: l1_last(4 + g))
                unit(C_IN + 48, nothing, lambda g, j: l1_state(8 + g, j), lambda g: l1_last(8 + g))

                act.wait_ge(n_out_ready, l1())
                for h in range(H):
                    act.dma_start(n_s[bass.ds(l, 1), :, h, :].rearrange("a b k -> (a b) k"),
                                  n_out[h * NS:(h + 1) * NS, :]).then_inc(n_stored, 16)
                act.wait_ge(columns_done, l * H + H)
                for n in range(2 * H):
                    act.wait_ge(cp_done, l * (2 * H) + (n + 1))
                    if n == 2:
                        act.wait_ge(columns_read, l1())
                        act.activation(head_ms[:, :, :], head_ms[:, :, :], ACT.Sqrt, bias=eps[:, 0:1],
                                       scale=1.0 / DV).then_inc(head_root, 1)
                    if n >= 2:
                        act.wait_ge(stage_stored[n % 2], 1 + l * (16 * STAGE_STORES) + 16 * (n // 2))
                    act.activation(stage[:, n % 2, :], ps[:, T_BANK + n % 2, :], ACT.Copy).then_inc(cp_copied, 1)
                    act.wait_ge(cp_copied, l * (2 * H) + (n + 1))
                    act.dma_start(c_p[bass.ds(l, 1), 0, n // 2, (n % 2) * P:(n % 2 + 1) * P, :].rearrange("a p v -> p (a v)"),
                                  stage[:, n % 2, :]).then_inc(stage_stored[n % 2], 16)
                act.wait_ge(npt_copied, l1())
                act.dma_start(n_p[bass.ds(l, 1), 0].rearrange("a h (kt p) -> (a h kt) p", p=P), np_row).then_inc(n_stored, 16)
                act.wait_ge(tail_copied, l1())
                act.dma_start(conv_p[bass.ds(l, 1), 0].rearrange("a r d -> (a r) d"),
                              stage[0:2, :, :].rearrange("p a b -> p (a b)")).then_inc(stage_stored[0], 16)
                act.dma_start(conv_s[bass.ds(l, 1), :, 1, :].rearrange("a b d -> (a b) d"),
                              stage[2:2 + NS, :, :].rearrange("p a b -> p (a b)")).then_inc(stage_stored[1], 16)

                def gate_evac(dst):
                    def evac(g):
                        act.activation(dst(g), pair[g % 2], ACT.Sigmoid).then_inc(pair_free[g % 2], 1)
                    return evac

                act.wait_ge(n_stored, 1 + l * (16 * (H + 1)) + 16 * (H + 1))
                with act.Fori(0, 2) as i:
                    def o_evac(g):
                        act.wait_ge(b_ready, 1 + l * 9 + (i * 4 + g))
                        act.activation(act_tmp[:, :, :], pair[g % 2], ACT.Sigmoid).then_inc(pair_free[g % 2], 1)
                    unit(i * 8 + (C_IN + 56), o_evac, *samples(i, 12))
                with act.Fori(0, 2) as i:
                    unit(i * 8 + (C_IN + 72), gate_evac(lambda g: QK[:, bass.ds(i * 8 + 2 * g, 2), :]), *samples(i, 20))

                with act.Fori(0, 2) as i:
                    for x in range(2):
                        scale_c(i * 2 + (28 + x), x, i + 6, NS - 1, i * 2 + x)
                        for j in range(2):
                            ahead(l, i * 4 + (C_PA + 2 * x + j), 2 * x + j)
                        store_c(i * 2 + (28 + x), x, NS - 1, i * 2 + x)
                act.wait_ge(hs_sum, l1())
                act.activation(r_den[:, :, :], den_s, ACT.Sqrt, bias=eps[:, 0:1], scale=1.0 / DV).then_inc(hs_root, 1)
                with act.Fori(0, 4) as i:
                    for j in range(4):
                        ahead(l, i * 4 + (C_PB + j), j)
                for g in range(4):
                    for j in range(2):
                        ahead(l, C_WO + 2 * g + j, 2 * g + j)
                    squares(l, g, G_WO + g)
                norm_root_of(l, 2)
                norm_hi(l, 2)
                ffn(l, 1, C_FFN2, G_FFN2)
                norm_n[0] = 0

            norm_root_of(DEPTH, 0)
            for s in range(3):
                act.wait_ge(y_copied, 2 * (s + 1))
                dst, n = ((y_prompt[0, 0:P, :], P), (y_prompt[0, P:2 * P, :], P), (y_sample[:, 0, :], NS))[s]
                act.dma_start(dst, y_rows[0:n, s, :]).then_inc(stored, 16)
            act.wait_ge(stored, 16 * 3)
            act.wait_ge(small_loaded, DEPTH * 16 * SMALL_LOADS)
            act.wait_ge(m_stored, 1 + DEPTH * 16 * 2)
            for s in range(2):
                act.wait_ge(stage_stored[s], 1 + DEPTH * 16 * STAGE_STORES)
            act.wait_ge(n_stored, 1 + DEPTH * 16 * (H + 1))
            for s in range(6):
                act.wait_ge(c_stored[s], 1 + DEPTH * 16 * PER_SLOT[s])

        @block.vector
        def _(dve):
            TT, STT, TS = dve.tensor_tensor, dve.scalar_tensor_tensor, dve.tensor_scalar
            norm_n = [0]

            def ahead(l, c, j):
                dve_split(dve, l, c + AHEAD, (j + AHEAD) % SLOTS)

            def wait_group(l, c_end):
                dve.wait_ge(chunk_done, 1 + l * CHUNKS + c_end)

            def add_squares(l, q):
                n = norm_n[0]
                norm_n[0] += 1
                dve.wait_ge(sq_ready, l * (4 * NORMS) + (n + 1))
                if q:
                    if q > 1:
                        dve.wait_ge(sums_ready, l * (3 * NORMS) + (n // 4 * 3 + q - 1))
                    TT(sq_sum[:, :, :], sq_sum[:, :, :], sq[:, :, :], ALU.add).then_inc(sums_ready, 1)

            def norm_scale(l, n, off):
                dve.wait_ge(norm_root, l * NORMS + (n + 1))
                dve.reciprocal(rstd[:, :], rstd[:, :])
                dve.drain()

                def lo_of(q):
                    dve.wait_ge(operand_hi, l * (4 * NORMS) + (4 * n + q + 1))
                    TT(A_l[:, 2 * q:2 * q + 2, :], (val, val2)[q % 2][:, :, :], A_h[:, 2 * q:2 * q + 2, :].bitcast(F32),
                       ALU.subtract).then_inc(operand_ready, 2)

                for q in range(4):
                    if q >= 2:
                        lo_of(q - 2)
                        dve.drain()
                    for f in range(2):
                        k = 2 * q + f
                        ins = STT((val, val2)[q % 2][:, f, :], X[:, k, :], par_at(l, off + k), rstd[:, :], ALU.mult, ALU.mult)
                    ins.then_inc(operand_val, 1)
                lo_of(2)
                lo_of(3)

            def par_at(l, c):
                return par[:, bass.ds(l * PARS + c, 1)]

            def ffn(l, which, c0, g0):
                with dve.Fori(0, FFN_PAIRS) as i:
                    for j in range(4):
                        ahead(l, i * 4 + (c0 + j), j)
                    wait_group(l, i * 4 + (c0 + 4))
                    dve.wait_ge(pair_free[0], 1 + l * (GROUPS // 2) + (i + (g0 // 2 + 1)))
                    TT(val[:, :, :], act_tmp[:, :, :], pair[1], ALU.mult).then_inc(pair_free[1], 1)
                    dve.wait_ge(hidden_hi, l * (2 * FFN_PAIRS) + (i + (which * FFN_PAIRS + 1)))
                    TT(G_l[:, bass.ds(i * 2, 2), :], val[:, :, :], G_h[:, bass.ds(i * 2, 2), :].bitcast(F32),
                       ALU.subtract).then_inc(hidden_ready, 1)
                for g in range(DOWN_GROUPS):
                    for j in range(DOWN_CHUNKS):
                        c = c0 + C_DOWN + g * DOWN_CHUNKS + j
                        if c + AHEAD < CHUNKS:
                            ahead(l, c, c)
                    wait_group(l, c0 + C_DOWN + (g + 1) * DOWN_CHUNKS)
                    STT(X[:, 2 * g:2 * g + 2, :], pair[g % 2], 0.5, X[:, 2 * g:2 * g + 2, :],
                        ALU.mult, ALU.add).then_inc(pair_free[g % 2], 1)
                    add_squares(l, g)

            dve.memset(ones[:, :], 1.0).then_inc(split_lo, SLOTS)
            dve.wait_ge(const_ready, 1)
            TT(pick[:, :], ident[:, 0:NS], ident[:, 32:32 + NS], ALU.add).then_inc(prep_copied, 1)
            dve.wait_ge(prep_tr, 1)
            dve.tensor_copy(par[:, :], ps[:, 4, 0:DEPTH * PARS + KT])
            for s in range(3):
                dve.wait_ge(prep_tr, s + 2)
                n = P if s < 2 else NS
                for half in range(2):
                    ins = dve.tensor_copy(X[:, 4 * half:4 * half + 4, s * P:s * P + n],
                                          ps[:, 2 * (s % 2) + half, 0:4 * n].rearrange("p (k t) -> p k t", k=4))
                ins.then_inc(prep_copied, 1)
            dve.drain()
            for q in range(4):
                add_squares(0, q)
            norm_n[0] = 0

            with dve.Fori(0, DEPTH) as l:
                def l1(c=0):
                    return l + (1 + c)

                for c in range(AHEAD):
                    dve_split(dve, l, c, c)
                norm_scale(l, 0, PAR_FFN1)
                norm_n[0] = 4
                ffn(l, 0, 0, 0)

                dve.wait_ge(wg_hi, l1())
                for part, w0 in enumerate((0, 32)):
                    at = [t[:, 0:KT * 36].rearrange("p (k c) -> p k c", c=36)[:, :, w0:w0 + H] for t in (wg_l, wg_h)]
                    ins = TT(at[0], wg[:, :, part * H:part * H + H], at[1].bitcast(F32), ALU.subtract)
                ins.then_inc(wg_ready, 1)
                norm_scale(l, 1, PAR_MIX)
                dve.wait_ge(gates_done, l1())
                TS(gate_i, ps[0:H, T_BANK, 0:T], bias_i[:, bass.ds(l, 1)], None, ALU.add)
                dve.tensor_copy(gate_f, ps[32:32 + H, T_BANK, 0:T])
                dve.drain()
                TS(gate_f, gate_f, bias_f[:, bass.ds(l, 1)], None, ALU.add)
                dve.drain()
                TS(gate_mn, gate_f, 0.0, None, ALU.min)
                dve.drain()
                STT(gate_na, gate_mn, 2.0, gate_f, ALU.mult, ALU.subtract).then_inc(gate_exp_in, 1)
                dve.wait_ge(gate_log, l1())
                TT(gate_lf, gate_mn, gate_ln, ALU.subtract)
                dve.drain()
                dve.tensor_tensor_scan(gate_b, ones[0:H, 0:1].broadcast_to([H, NP]), gate_lf[:, 0:NP], 0.0, ALU.mult, ALU.add)
                dve.drain()
                TT(aw[:, 0, :], gate_i[:, 0:NP], gate_b, ALU.subtract)
                dve.drain()
                dve.tensor_tensor_scan(gate_mx, aw[:, 0, :], aw[:, 0, :], 0.0, ALU.max, ALU.max)
                TT(s_inter, gate_lf[:, NP:T], m_old[:, :], ALU.add)
                dve.drain()
                dve.wait_ge(m_stored, 1 + l * 32)
                TS(rows[:, 0, :], gate_mx, -1.0, None, ALU.mult)
                TT(rows[:, 1, :], gate_b, gate_mx, ALU.add)
                TT(m_new[:, :], s_inter, gate_i[:, NP:T], ALU.max)
                dve.drain()
                TT(s_rows[:, 0, :], s_inter, m_new[:, :], ALU.subtract)
                TT(s_rows[:, 1, :], gate_i[:, NP:T], m_new[:, :], ALU.subtract)
                TS(s_rows[:, 2, :], m_new[:, :], -1.0, None, ALU.mult).then_inc(gate_rows, 1)

                def unit(c0, evac, sample=lambda g, s: None, last=lambda g: None):
                    for g in range(4):
                        for j in range(2):
                            sample(g, j)
                            ahead(l, c0 + 2 * g + j, 2 * g + j)
                        if evac:
                            wait_group(l, c0 + 2 * g + 2)
                            evac(g)
                        last(g)

                with dve.Fori(0, 2) as i:
                    unit(i * 8 + C_IN, None)
                dve.wait_ge(small_done, l1())
                dve.tensor_copy(small[:, :], ps[:, T_BANK, 0:SM_END]).then_inc(small_copied, 1)
                dve.drain()
                for p in range(2):
                    dve.wait_ge(pair_free[p], 1 + l * (GROUPS // 2) + (ORDER_G["v0"] // 2))
                TS(q_s[:, :, :, :].rearrange("p h k b -> p (h k) b"), QK[:, 0:KT, NP:T], DK ** -0.5, None, ALU.mult)
                for kt in range(KPH):
                    TT(wk_s[:, :, kt, :], QK[:, KT + kt:2 * KT:KPH, NP:T], s_bc[:, :, 1, :], ALU.mult)
                    TT(n_new[:, kt, :, :], n_t[:, kt, :, :].rearrange("p b h -> p h b"), s_bc[:, :, 0, :], ALU.mult)
                dve.drain()
                for kt in range(KPH):
                    TT(n_new[:, kt, :, :], n_new[:, kt, :, :], wk_s[:, :, kt, :], ALU.add)
                dve.drain()
                for kt in range(KPH):
                    TT(qn[:, kt, :, :], n_new[:, kt, :, :], q_s[:, :, kt, :], ALU.mult)
                dve.drain()
                TT(qn_sum[:, :, :], qn[:, 0, :, :], qn[:, 1, :, :], ALU.add).then_inc(qn_ready, 1)
                with dve.Fori(0, 2) as i:
                    unit(i * 8 + (C_IN + 16), None)

                def sample_state(n, s, b, h):
                    dve.wait_ge(c_scaled, l * (NS * H) + (n + 1))
                    dve.wait_ge(vbc_done, l * (NS * H) + (n + 1))
                    for kt in range(KPH):
                        w = wk_s[:, bass.ds(h, 1), kt, b:b + 1].rearrange("p a c -> p (a c)")
                        ins = STT(C[s][:, kt, :], ps[:, V_BANK, :], w, C[s][:, kt, :], ALU.mult, ALU.add)
                    ins.then_inc(c_new, 1)

                def samples(i, n0):
                    return lambda g, j: sample_state(i * 4 + (n0 + g), 2 + g, g, i + (n0 - 12) // 4) if j == 0 else None

                def l1_state(i, j):
                    for n in l1_states(i, j):
                        sample_state(n, n % 2, 4 + n // H, n % H)

                def v_row_lo(t):
                    dve.wait_ge(v_hi, l * 4 + (t - 11))
                    cols = slice((t - 12) * 512, (t - 11) * 512)
                    TT(v_rows[32:32 + NS, cols], ps[0:NS, T_BANK + t % 2, :], v_rows[0:NS, cols].bitcast(F32),
                       ALU.subtract).then_inc(tr_free[t % 2], 1)

                def head_decay(h):
                    dve.wait_ge(score_done, l * H + (h + 1))
                    STT(decay[:, 0:NP], ps[:, T_BANK + 1, 0:NP], aw_t[:, 0, 0, h:h + 1], causal[:, :], ALU.add, ALU.min)
                    STT(decay[:, NP:NP + P], ps[:, T_BANK + 1, P:NP], aw_t[:, 0, 1, h:h + 1], causal[:, 0:P],
                        ALU.add, ALU.min).then_inc(decay_arg, 1)
                    for st in range(2):
                        kk = k_tok[:, st, h * DK:(h + 1) * DK]
                        TS(kk, kk, aw_t[:, 1, st, h:h + 1], None, ALU.mult)
                    dve.wait_ge(decay_ready, l * H + (h + 1))
                    STT(score, ps[:, T_BANK, 0:NP + P], DK ** -0.5, decay, ALU.mult, ALU.mult).then_inc(score_ready, 1)

                def head_factors():
                    dve.wait_ge(columns_done, l * H + H)
                    TT(head_den[:, :, :], den_c, aw_t[:, 2, :, :], ALU.max)
                    dve.tensor_copy(head_ms[:, :, :], ms_c)
                    dve.drain()
                    STT(head_den[:, :, :], den_c, -1.0, head_den[:, :, :], ALU.mult, ALU.max)
                    dve.drain()
                    dve.reciprocal(head_den[:, :, :], head_den[:, :, :])
                    dve.drain()
                    TT(head_ms[:, :, :], head_ms[:, :, :], head_den[:, :, :], ALU.mult)
                    dve.drain()
                    TT(head_ms[:, :, :], head_ms[:, :, :], head_den[:, :, :], ALU.mult).then_inc(columns_read, 1)
                    dve.wait_ge(head_root, l1())
                    dve.reciprocal(head_f[:, :, :], head_ms[:, :, :])
                    dve.drain()
                    TT(head_f[:, :, :], head_f[:, :, :], head_den[:, :, :], ALU.mult)
                    for half in range(2):
                        if half == 0:
                            dve.drain()
                        for x in range(4):
                            ins = TS(diag[half][:, x, :], ident[:, :], head_f[:, x % 2, 2 * half + x // 2:2 * half + x // 2 + 1], None, ALU.mult)
                        ins.then_inc(diag_ready, 1)

                def head_scale():
                    for h in range(H):
                        dve.wait_ge(factors_done, l * 2 + (h // 2 + 1))
                        t = VH[:, VPH * h:VPH * (h + 1), 0:NP]
                        f = ps[:, T_BANK + h // 2:T_BANK + h // 2 + 1, (h % 2) * NP:(h % 2 + 1) * NP]
                        TT(t, t, f.broadcast_to([P, VPH, NP]), ALU.mult)
                    dve.drain()

                def sample_den():
                    dve.wait_ge(den_done, l1())
                    d = den_s.rearrange("p (h b) -> p h b", h=H)
                    TT(r_den[:, :, :], d, s_bc[:, :, 2, :], ALU.max)
                    dve.drain()
                    STT(r_den[:, :, :], d, -1.0, r_den[:, :, :], ALU.mult, ALU.max)
                    dve.drain()
                    dve.reciprocal(r_den[:, :, :], r_den[:, :, :])
                    dve.wait_ge(n_stored, 1 + l * (16 * (H + 1)))
                    dve.tensor_copy(n_out, n_rows_ps).then_inc(n_out_ready, 1)

                def l1_last(i):
                    if i == 3:
                        for t in range(12, 16):
                            v_row_lo(t)
                        sample_den()
                    if i >= 3 and i % 2 == 1 and i < 11:
                        head_decay((i - 3) // 2)

                def xa_evac(g):
                    TT(U[:, 2 * g:2 * g + 2, :], U[:, 2 * g:2 * g + 2, :], pair[g % 2], ALU.mult).then_inc(pair_free[g % 2], 1)
                    dve.drain()
                    dve.tensor_copy(u_keep[:, 2 * g:2 * g + 2, :], U[:, 2 * g:2 * g + 2, NP - 2:T])

                def gb_evac(g):
                    for f in range(2):
                        k = 2 * g + f
                        w = [par_at(l, PAR_CONV + KT * j + k) for j in range(3)]
                        TS(val[:, f, :], U[:, k, :], w[2], None, ALU.mult)
                    for j in (1, 0):
                        dve.drain()
                        for f in range(2):
                            k = 2 * g + f
                            w = par_at(l, PAR_CONV + KT * j + k)
                            t = val[:, f, 2 - j:NP]
                            STT(t, U[:, k, 0:NP - 2 + j], w, t, ALU.mult, ALU.add)
                            t = val[:, f, NP:T]
                            STT(t, cv_t[:, k, :, j], w, t, ALU.mult, ALU.add)
                    dve.drain()
                    TT(U[:, 2 * g:2 * g + 2, :], val[:, :, :], pair[g % 2], ALU.mult).then_inc(pair_free[g % 2], 1)

                unit(C_IN + 32, None, last=l1_last)
                unit(C_IN + 40, xa_evac, lambda g, j: l1_state(4 + g, j), lambda g: l1_last(4 + g))
                unit(C_IN + 48, gb_evac, lambda g, j: l1_state(8 + g, j), lambda g: l1_last(8 + g))

                dve.wait_ge(np_done, l1())
                dve.tensor_copy(np_col[:, :], np_ps).then_inc(np_copied, 1)
                head_factors()
                dve.wait_ge(npt_done, l1())
                dve.tensor_copy(np_row, npt_ps).then_inc(npt_copied, 1)
                dve.wait_ge(tail_done, l1())
                for s in range(2):
                    dve.wait_ge(stage_stored[s], 1 + l * (16 * STAGE_STORES) + 16 * H)
                dve.tensor_copy(stage[0:2 + NS, :, :], ps[0:2 + NS, T_BANK:T_BANK + 2, :]).then_inc(tail_copied, 1)
                head_scale()

                with dve.Fori(0, 2) as i:
                    def o_evac(g):
                        tile = i * 8 + 2 * g
                        dve.wait_ge(pair_free[g % 2], 1 + l * (GROUPS // 2) + (i * 2 + (ORDER_G["o0"] // 2 + g // 2 + 1)))
                        for f in range(2):
                            w = par[:, bass.ds(l * PARS + (i * 8 + (PAR_HEAD + 2 * g + f)), 1)]
                            STT(val[:, f, 0:NP], act_tmp[:, f, 0:NP], w,
                                VH[:, bass.ds(tile + f, 1), 0:NP].rearrange("p a t -> p (a t)"), ALU.mult, ALU.mult)
                            TS(gate_s[:, bass.ds(tile + f, 1), :].rearrange("p a b -> p (a b)"), act_tmp[:, f, NP:T], w, None, ALU.mult)
                        dve.drain()
                        dve.tensor_copy(B_h[:, bass.ds(tile, 2), 0:NP], val[:, :, 0:NP])
                        dve.drain()
                        TT(B_l[:, bass.ds(tile, 2), 0:NP], val[:, :, 0:NP], B_h[:, bass.ds(tile, 2), 0:NP].bitcast(F32),
                           ALU.subtract).then_inc(b_ready, 1)
                    unit(i * 8 + (C_IN + 56), o_evac, samples(i, 12))
                with dve.Fori(0, 2) as i:
                    unit(i * 8 + (C_IN + 72), None, samples(i, 20))

                wait_group(l, C_PA)
                for q in range(4):
                    dve.tensor_copy(A_h[:, 2 * q:2 * q + 2, :], U[:, 2 * q:2 * q + 2, :])
                dve.drain()
                for q in range(4):
                    TT(A_l[:, 2 * q:2 * q + 2, :], U[:, 2 * q:2 * q + 2, :], A_h[:, 2 * q:2 * q + 2, :].bitcast(F32),
                       ALU.subtract).then_inc(operand_ready, 2)

                def pa_evac(g):
                    dst = GA[:, bass.ds(i * 4 + 2 * g, 2), :]
                    TT(dst, dst, pair[g % 2], ALU.mult).then_inc(pair_free[g % 2], 1)

                with dve.Fori(0, 2) as i:
                    for g in range(2):
                        sample_state(i * 2 + (28 + g), g, NS - 1, i * 2 + g)
                        for j in range(2):
                            ahead(l, i * 4 + (C_PA + 2 * g + j), 2 * g + j)
                        wait_group(l, i * 4 + (C_PA + 2 * g + 2))
                        pa_evac(g)
                dve.wait_ge(num_done, l * (NS * H) + (NS * H + 2))
                for v in range(VPH):
                    TT(h_s[:, :, v, :], num_s[:, :, v, :], r_den[:, :, :], ALU.mult)
                dve.drain()
                TT(h_sq[:, :, :, :], h_s[:, :, :, :], h_s[:, :, :, :], ALU.mult)
                dve.drain()
                for v in range(1, VPH - 1):
                    TT(h_sum[:, :, :], h_sq[:, :, v, :], h_sq[:, :, 0, :] if v == 1 else h_sum[:, :, :], ALU.add)
                    dve.drain()
                TT(h_sum[:, :, :], h_sum[:, :, :], h_sq[:, :, VPH - 1, :], ALU.add).then_inc(hs_sum_ready, 1)

                dve.wait_ge(hs_root, l1())
                dve.reciprocal(h_sum[:, :, :], r_den[:, :, :])
                dve.drain()
                for v in range(VPH):
                    TT(h_s[:, :, v, :], h_s[:, :, v, :], h_sum[:, :, :], ALU.mult)
                dve.drain()
                hs_f = h_s[:, :, :, :].rearrange("p h v b -> p (h v) b")
                TT(hs_f, hs_f, gate_s[:, :, :], ALU.mult)
                dve.drain()
                dve.tensor_copy(B_h[:, :, NP:T], hs_f)
                dve.drain()
                TT(B_l[:, :, NP:T], hs_f, B_h[:, :, NP:T].bitcast(F32), ALU.subtract).then_inc(b_ready, 1)

                def mix(g, idx):
                    TT(val[:, :, :], GM[:, idx, :], pair[g % 2], ALU.mult).then_inc(pair_free[g % 2], 1)
                    dve.drain()
                    TT(val[:, :, :], val[:, :, :], GA[:, idx, :], ALU.add)
                    dve.drain()
                    dve.tensor_copy(A_h[:, idx, :], val[:, :, :])
                    dve.drain()
                    TT(A_l[:, idx, :], val[:, :, :], A_h[:, idx, :].bitcast(F32), ALU.subtract).then_inc(operand_ready, 2)

                for g in range(4):
                    for j in range(4):
                        ahead(l, C_PB + 4 * g + j, j)
                    wait_group(l, C_PB + 4 * g + 4)
                    mix(g, slice(2 * g, 2 * g + 2))
                for g in range(4):
                    for j in range(2):
                        ahead(l, C_WO + 2 * g + j, 2 * g + j)
                    wait_group(l, C_WO + 2 * g + 2)
                    TT(X[:, 2 * g:2 * g + 2, :], X[:, 2 * g:2 * g + 2, :], pair[g % 2], ALU.add).then_inc(pair_free[g % 2], 1)
                    add_squares(l, g)
                norm_scale(l, 2, PAR_FFN2)
                ffn(l, 1, C_FFN2, G_FFN2)
                norm_n[0] = 0

            dve.wait_ge(norm_root, DEPTH * NORMS + 1)
            dve.reciprocal(rstd[:, :], rstd[:, :])
            dve.drain()
            for k in range(KT):
                STT(U[:, k, :], X[:, k, :], par[:, DEPTH * PARS + k:DEPTH * PARS + k + 1], rstd[:, :],
                    ALU.mult, ALU.mult).then_inc(y_tiles, 1)
            for s in range(3):
                n = P if s < 2 else NS
                for half in range(2):
                    dve.wait_ge(y_tr, 2 * s + half + 1)
                    dve.tensor_copy(y_rows[0:n, s, half * 512:(half + 1) * 512], ps[0:n, T_BANK + half, :]).then_inc(y_copied, 1)

        @block.tensor
        def _(pe):
            def product(l, c, slot, n, out, src_h, src_l, k0, first, last, then=None):
                pe.wait_ge(split_lo, l * CHUNKS + (c + (SLOTS + 1)))
                w_h = hi[slot][:, 0:n * GW].rearrange("p (k n) -> p k n", n=GW)
                w_l = lo[slot][:, 0:n * GW].rearrange("p (k n) -> p k n", n=GW)
                for f in range(2):
                    cols = slice(f * P, (f + 1) * P)
                    for k in range(n):
                        a, z = first and k == 0, last and k == n - 1
                        pe.matmul(out[:, f, :], w_h[:, k, cols], src_h[:, k0 + k, :], start=a, stop=False)
                        pe.matmul(out[:, f, :], w_h[:, k, cols], src_l[:, k0 + k, :], start=False, stop=False)
                        ins = pe.matmul(out[:, f, :], w_l[:, k, cols], src_h[:, k0 + k, :], start=False, stop=z)
                ins.then_inc(chunk_done, 1)

            def group_free(l, g2, p):
                pe.wait_ge(pair_free[p], 1 + l * (GROUPS // 2) + g2)

            def operand(l, n):
                pe.wait_ge(operand_ready, l * OPS + n)

            def norm_sums(l, n):
                pe.wait_ge(sums_ready, l * (3 * NORMS) + 3 * (n + 1))
                for f in range(2):
                    ins = pe.matmul(ps[:, 7, 0:T], ones[:, :], sq_sum[:, f, :], start=f == 0, stop=f == 1)
                ins.then_inc(norm_sum, 1)

            def ffn(l, which, c0, g0, op):
                with pe.Fori(0, FFN_PAIRS) as i:
                    for g in range(2):
                        group_free(l, i + g0 // 2, g)
                        for j in range(2):
                            operand(l, op + CK * (j + 1))
                            product(l, i * 4 + (c0 + 2 * g + j), 2 * g + j, CK, pair[g], A_h, A_l, CK * j, j == 0, j == 1)
                with pe.Fori(0, DOWN_GROUPS // 2) as i:
                    for g in range(2):
                        group_free(l, i + (g0 // 2 + FFN_PAIRS), g)
                        for j in range(DOWN_CHUNKS):
                            n = min(CK, FT - CK * j)
                            pe.wait_ge(hidden_ready, l * (2 * FFN_PAIRS) + (which * FFN_PAIRS + (CK * j + n) // 2))
                            s = (g * DOWN_CHUNKS + j) % SLOTS
                            product(l, i * (2 * DOWN_CHUNKS) + (c0 + C_DOWN + g * DOWN_CHUNKS + j), s, n,
                                    pair[g], G_h, G_l, CK * j, j == 0, j == DOWN_CHUNKS - 1)

            pe.wait_ge(const_ready, 1)
            pe.wait_ge(prep_loaded, 16 * PREP_LOADS)
            pe.transpose(ps[:, 4, 0:P], par_rows, ident[:, :])
            pe.transpose(ps[:, 4, P:P + KT], gf_rows, ident[0:KT, 0:KT]).then_inc(prep_tr, 1)
            for s in range(3):
                n = P if s < 2 else NS
                if s == 2:
                    pe.wait_ge(prep_copied, 2)
                for k in range(KT):
                    src = x_rows[:, s, k * P:(k + 1) * P] if s < 2 else xs_rows[:, k * P:(k + 1) * P]
                    ins = pe.transpose(ps[:, 2 * (s % 2) + k // 4, (k % 4) * n:(k % 4 + 1) * n], src, ident[0:n, 0:n])
                ins.then_inc(prep_tr, 1)
            pe.wait_ge(prep_copied, 4)
            pe.transpose(ps[0:KT, 4, 0:KT], gf_rows[:, 0:KT], ident[0:KT, 0:KT]).then_inc(num_done, 2)

            with pe.Fori(0, DEPTH) as l:
                def l1(c=0):
                    return l + (1 + c)

                norm_sums(l, 0)
                ffn(l, 0, 0, 0, OP_NORM1)
                norm_sums(l, 1)

                pe.wait_ge(wg_ready, l1())
                operand(l, OP_NORM2 + KT)
                for k in range(KT):
                    cols = slice(36 * k, 36 * k + P)
                    o = ps[:, T_BANK, 0:T]
                    pe.matmul(o, wg_h[:, cols], A_h[:, k, :], start=k == 0, stop=False)
                    pe.matmul(o, wg_h[:, cols], A_l[:, k, :], start=False, stop=False)
                    ins = pe.matmul(o, wg_l[:, cols], A_h[:, k, :], start=False, stop=k == KT - 1)
                ins.then_inc(gates_done, 1)

                def unit(c0, g0, before=lambda g, s: None, after=lambda g, s: None, end=lambda g: None):
                    for g in range(4):
                        for j in range(2):
                            before(g, j)
                            if j == 0:
                                group_free(l, g0 + g // 2, g % 2)
                            product(l, c0 + 2 * g + j, (2 * g + j) % SLOTS, CK, pair[g % 2], A_h, A_l, CK * j, j == 0, j == 1)
                            after(g, j)
                        end(g)

                with pe.Fori(0, 2) as i:
                    unit(i * 8 + C_IN, i * 2 + G_IN // 2)

                pe.wait_ge(gate_exps, l1())
                pe.wait_ge(small_loaded, l * (16 * SMALL_LOADS) + 16 * SMALL_LOADS)
                own_step(pe)
                for kind in range(3):
                    for st in range(2):
                        at = SM_AW + kind * 8 + st * 4
                        pe.transpose(ps[:, T_BANK, at:at + H], aw[:, kind, st * P:(st + 1) * P], ident[0:H, 0:H])
                for h in range(H):
                    at = SM_S + 24 * h
                    pe.matmul(ps[:, T_BANK, at:at + 24], ident[0:H, h:h + 1].broadcast_to([H, P]),
                              s_rows[:, :, :], start=True, stop=True)
                for kt in range(KPH):
                    at = SM_N + 32 * kt
                    pe.transpose(ps[:, T_BANK, at:at + 32], n_old[:, kt * P:(kt + 1) * P], ident[0:NS * H, 0:NS * H])
                for k in range(KT):
                    at = SM_CV + 16 * k
                    ins = pe.transpose(ps[:, T_BANK, at:at + 16], conv_rows[:, k * P:(k + 1) * P], ident[0:2 * NS, 0:2 * NS])
                ins.then_inc(small_done, 1)

                with pe.Fori(0, 2) as i:
                    unit(i * 8 + (C_IN + 16), i * 2 + ORDER_G["v0"] // 2)

                def tokens(t):
                    if t < 2:
                        pe.wait_ge(small_copied, l1())
                    pe.wait_ge(tr_free[t % 2], 1 + l * 8 + t // 2)
                    for x in range(4):
                        if t < 4:
                            src = QK[:, KT + (t // 2) * 4 + x, (t % 2) * P:(t % 2 + 1) * P]
                        elif t < 12:
                            src = VH[:, ((t - 4) // 2) * 4 + x, (t % 2) * P:(t % 2 + 1) * P]
                        else:
                            src = VH[:, (t - 12) * 4 + x, NP:T]
                        rows_n = P if t < 12 else NS
                        ins = pe.transpose(ps[0:rows_n, T_BANK + t % 2, x * P:(x + 1) * P], src, ident[:, :])
                    ins.then_inc(tr_done, 1)

                def scores(h):
                    if h == 0:
                        for p in range(2):
                            pe.wait_ge(tr_free[p], 1 + l * 8 + 8)
                    else:
                        pe.wait_ge(av_read, l * H + h)
                    for st in range(2):
                        for kt in range(KPH):
                            pe.matmul(ps[:, T_BANK, st * NP:st * NP + NP - st * P],
                                      QK[:, KT + h * KPH + kt, st * P:(st + 1) * P],
                                      QK[:, h * KPH + kt, st * P:NP], start=kt == 0, stop=kt == KPH - 1)
                    pe.matmul(ps[:, T_BANK + 1, 0:NP], ident[0:H, h:h + 1].broadcast_to([H, P]),
                              rows[:, 0, :], start=True, stop=True).then_inc(score_done, 1)

                def values(h):
                    pe.wait_ge(score_ready, l * H + (h + 1))
                    for v in range(VPH):
                        out = ps[:, T_BANK + v // 2, (v % 2) * NP:(v % 2 + 1) * NP]
                        for st in range(2):
                            w = v_tok[:, st, h * DV + v * P:h * DV + (v + 1) * P]
                            ins = pe.matmul(out[:, st * P:NP], w, score[:, st * NP:st * NP + NP - st * P],
                                            start=st == 0, stop=st == 1)
                    ins.then_inc(av_done, 1)
                    for tt in range(2):
                        for st in range(tt + 1):
                            at = st * NP + (tt - st) * P
                            pe.matmul(den_c[:, tt, h:h + 1], score[:, at:at + P], ones[:, 0:1], start=st == 0, stop=st == tt)

                def head_columns(h):
                    pe.wait_ge(av_read, l * H + (h + 1))
                    for tt in range(2):
                        for v in range(VPH):
                            at = (v % 2) * NP + tt * P
                            ins = pe.matmul(ms_c[:, tt, h:h + 1], stage[:, v // 2, at:at + P], ones[:, 0:1],
                                            start=v == 0, stop=v == VPH - 1)
                    ins.then_inc(columns_done, 1)

                def broadcast_v(n, b, h):
                    pe.wait_ge(c_new, 1 + l * (NS * H) + n)
                    pe.matmul(ps[:, V_BANK, :], pick[:, b:b + 1].broadcast_to([P, P]),
                              v_rows[:, bass.ds(h * DV, DV)], start=True, stop=True).then_inc(vbc_done, 1)

                def numerator(n, s, b, h):
                    pe.wait_ge(c_new, 1 + l * (NS * H) + (n + 1))
                    for v in range(VPH):
                        for kt in range(KPH):
                            out = num_s[:, bass.ds(h, 1), v, b:b + 1].rearrange("p a c -> p (a c)")
                            q = q_s[:, bass.ds(h, 1), kt, b:b + 1].rearrange("p a c -> p (a c)")
                            ins = pe.matmul(out, C[s][:, kt, v * P:(v + 1) * P], q, start=kt == 0, stop=kt == KPH - 1)
                    ins.then_inc(num_done, 1)

                def sample_den():
                    pe.wait_ge(qn_ready, l1())
                    pe.matmul(den_s, ones[:, :], qn_sum[:, :, :], start=True, stop=True)
                    for kt in range(KPH):
                        ins = pe.transpose(n_rows_ps[:, kt * P:(kt + 1) * P], n_new[:, kt, :, :].rearrange("p h b -> p (h b)"), ident[:, :])
                    ins.then_inc(den_done, 1)

                def samples(i, n0):
                    h = i + (n0 - 12) // 4
                    return (lambda g, j: None if j else broadcast_v(i * 4 + (n0 + g), g, h),
                            lambda g, j: numerator(i * 4 + (n0 + g), 2 + g, g, h) if j else None)

                def l1_before(i, j):
                    for n in l1_states(i, j):
                        broadcast_v(n, 4 + n // H, n % H)

                def l1_after(i, j):
                    for n in l1_states(i, j) if i >= 8 else l1_states(i, 0) if j else ():
                        numerator(n, n % 2, 4 + n // H, n % H)

                def l1_end(i):
                    if i == 0:
                        for p in range(2):
                            pe.wait_ge(pair_free[p], 1 + l * (GROUPS // 2) + ORDER_G["gc"] // 2)
                    if i < 4:
                        for t in range(4 * i, 4 * i + 4):
                            tokens(t)
                    if i == 3:
                        sample_den()
                    if i >= 5 and i % 2 == 1:
                        head_columns((i - 5) // 2)
                    if i >= 3 and i % 2 == 1 and i < 11:
                        if i == 3:
                            pe.wait_ge(n_out_ready, l1())
                        scores((i - 3) // 2)
                    if i >= 4 and i % 2 == 0:
                        values((i - 4) // 2)

                unit(C_IN + 32, ORDER_G["gc"] // 2, end=l1_end)
                unit(C_IN + 40, ORDER_G["xa"] // 2, lambda g, j: l1_before(4 + g, j), lambda g, j: l1_after(4 + g, j),
                     lambda g: l1_end(4 + g))
                unit(C_IN + 48, ORDER_G["gb"] // 2, lambda g, j: l1_before(8 + g, j), lambda g, j: l1_after(8 + g, j),
                     lambda g: l1_end(8 + g))

                for n in range(H * KPH):
                    for st in range(2):
                        ins = pe.matmul(np_ps[:, n:n + 1], k_tok[:, st, n * P:(n + 1) * P], ones[:, 0:1], start=st == 0, stop=st == 1)
                ins.then_inc(np_done, 1)
                for n in range(H * KPH):
                    h = n // KPH
                    if n == 1:
                        pe.wait_ge(np_copied, l1())
                    if n >= 2:
                        pe.wait_ge(cp_copied, l * (2 * H) + (n - 1))
                    for st in range(2):
                        ins = pe.matmul(ps[:, T_BANK + n % 2, :], k_tok[:, st, n * P:(n + 1) * P],
                                        v_tok[:, st, h * DV:(h + 1) * DV], start=st == 0, stop=st == 1)
                    ins.then_inc(cp_done, 1)
                pe.transpose(npt_ps, np_col[:, :], ident[:, :]).then_inc(npt_done, 1)
                pe.wait_ge(cp_copied, l * (2 * H) + 2 * H)
                for k in range(KT):
                    ins = pe.transpose(ps[0:2 + NS, T_BANK + k // 4, (k % 4) * P:(k % 4 + 1) * P], u_keep[:, k, :], ident[:, :])
                ins.then_inc(tail_done, 1)
                pe.wait_ge(tail_copied, l1())
                for half in range(2):
                    pe.wait_ge(diag_ready, l * 2 + (half + 1))
                    for x in range(4):
                        ins = pe.matmul(ps[:, T_BANK + half, x * P:(x + 1) * P], ones[:, :], diag[half][:, x, :], start=True, stop=True)
                    ins.then_inc(factors_done, 1)

                with pe.Fori(0, 2) as i:
                    unit(i * 8 + (C_IN + 56), i * 2 + ORDER_G["o0"] // 2, *samples(i, 12))
                with pe.Fori(0, 2) as i:
                    unit(i * 8 + (C_IN + 72), i * 2 + ORDER_G["ga"] // 2, *samples(i, 20))

                with pe.Fori(0, 2) as i:
                    for g in range(2):
                        broadcast_v(i * 2 + (28 + g), NS - 1, i * 2 + g)
                        group_free(l, i + G_PA // 2, g)
                        for j in range(2):
                            operand(l, OP_YA + CK * (j + 1))
                            product(l, i * 4 + (C_PA + 2 * g + j), 2 * g + j, CK, pair[g], A_h, A_l, CK * j, j == 0, j == 1)
                        numerator(i * 2 + (28 + g), g, NS - 1, i * 2 + g)
                pe.wait_ge(hs_sum_ready, l1())
                pe.matmul(den_s, ones[:, :], h_sum[:, :, :], start=True, stop=True).then_inc(hs_sum, 1)
                pe.wait_ge(b_ready, 1 + l * 9 + 9)
                own_step(pe)
                with pe.Fori(0, 2) as i:
                    for g in range(2):
                        group_free(l, i + G_PB // 2, g)
                        for j in range(4):
                            product(l, i * 8 + (C_PB + 4 * g + j), j, CK, pair[g], B_h, B_l, CK * j, j == 0, j == 3)
                with pe.Fori(0, 2) as i:
                    for g in range(2):
                        group_free(l, i + G_WO // 2, g)
                        for j in range(2):
                            operand(l, OP_MIX + CK * (j + 1))
                            product(l, i * 4 + (C_WO + 2 * g + j), 2 * g + j, CK, pair[g], A_h, A_l, CK * j, j == 0, j == 1)
                norm_sums(l, 2)
                ffn(l, 1, C_FFN2, G_FFN2, OP_NORM3)

            norm_sums(DEPTH, 0)
            pe.wait_ge(y_tiles, KT)
            for s in range(3):
                n = P if s < 2 else NS
                for half in range(2):
                    if s:
                        pe.wait_ge(y_copied, 2 * (s - 1) + half + 1)
                    else:
                        pe.wait_ge(norm_root, DEPTH * NORMS + 1)
                    for k in range(4):
                        ins = pe.transpose(ps[0:n, T_BANK + half, k * P:(k + 1) * P], U[:, 4 * half + k, s * P:s * P + n], ident[:, :])
                    ins.then_inc(y_tr, 1)


INPUTS = ["x_prompt", "x_sample", "state_conv", "state_mlstm_c", "state_mlstm_n", "state_mlstm_m",
          "g_ffn1", "w_ffn1_gu", "w_ffn1_down", "g_mix", "w_in", "w_conv", "b_igate", "b_fgate", "g_head",
          "w_proj_a", "w_proj_b", "w_out", "g_ffn2", "w_ffn2_gu", "w_ffn2_down", "g_final"]
OUTPUTS = [(1, NP, D), (NS, 1, D), (DEPTH, 1, 2, D), (DEPTH, 1, H, DK, DV), (DEPTH, 1, H, DK), (DEPTH, 1, H),
           (DEPTH, NS, 2, D), (DEPTH, NS, H, DK, DV), (DEPTH, NS, H, DK), (DEPTH, NS, H)]


def kernel(**inputs):
    import numpy as np
    import concourse.bacc as bacc
    from concourse.bass_utils import run_bass_kernel_spmd as run

    nc = bacc.Bacc("TRN2", target_bir_lowering=False, num_devices=1, dynamic_dma_scratch_size=SCRATCH)
    arrays, args = {}, []
    for name in INPUTS:
        a = np.ascontiguousarray(inputs[name])
        arrays[f"in_{name}"] = a
        args.append(nc.dram_tensor(f"in_{name}", a.shape, mybir.dt.from_np(a.dtype), kind="ExternalInput").ap())
    for i, shape in enumerate(OUTPUTS):
        args.append(nc.dram_tensor(f"out_{i}", shape, F32, kind="ExternalOutput").ap())
    build_program(nc, *args)
    r = run(nc, [arrays], core_ids=[0])
    return tuple(r.results[0][f"out_{i}"] for i in range(len(OUTPUTS)))
```

```python
import concourse.bass as bass
from concourse import mybir
from contextlib import ExitStack

F32 = mybir.dt.float32
F32R = mybir.dt.float32r
ACT = mybir.ActivationFunctionType
ALU = mybir.AluOpType

P = 128
DEPTH = 2
D = 1024
NP, NS = 256, 8
T = NP + NS
H, DK, DV = 4, 256, 512
D_FF = 2816
EPS = 1e-6
KT = D // P
FT = D_FF // P
VT_TILES = H * DV // P
VPH = DV // P
KPH = DK // P
GATE_COL = 3 * D + 2 * H * DK + 2 * H * DV
SLOTS = 4
CK = 4
GW = 2 * P
CHUNK = CK * GW

FFN_PAIRS = D_FF // GW
DOWN_CHUNKS = -(-FT // CK)
DOWN_GROUPS = D // GW
C_DOWN = FFN_PAIRS * 4
FFN_CHUNKS = C_DOWN + DOWN_CHUNKS * DOWN_GROUPS
FFN_GROUPS = 2 * FFN_PAIRS + DOWN_GROUPS
UNIT_GROUPS = D // GW
C_IN = FFN_CHUNKS
C_PA = C_IN + 11 * UNIT_GROUPS * 2
C_PB = C_PA + 4 * 2
C_WO = C_PB + 4 * 4
C_FFN2 = C_WO + 4 * 2
CHUNKS = C_FFN2 + FFN_CHUNKS
G_IN = FFN_GROUPS
G_PA = G_IN + 11 * UNIT_GROUPS
G_PB = G_PA + 4
G_WO = G_PB + 4
G_FFN2 = G_WO + 4
GROUPS = G_FFN2 + FFN_GROUPS
assert CHUNKS % SLOTS == 0 and C_IN % SLOTS == 0 and GROUPS % 2 == 0 and G_IN % 2 == 0
SUMMED = 9
M_TILE = 2 * VT_TILES
WG_TILE = 2 * FT
assert M_TILE + 2 * KT >= WG_TILE + 4
SCRATCH = 2048
AHEAD = 3

U_GB, U_GC, U_XA, U_Q, U_O = 0, 1, 2, 3, 7
ORDER_G = {name: G_IN + UNIT_GROUPS * n for n, name in enumerate(["q", "k", "v0", "v1", "gc", "xa", "gb", "o0", "o1", "ga", "gm"])}

PAR_FFN1, PAR_MIX, PAR_FFN2, PAR_CONV, PAR_HEAD, PARS = 0, 8, 16, 24, 48, 64
OP_NORM1, OP_NORM2, OP_YA, OP_MIX, OP_NORM3, OPS = 0, 8, 16, 24, 32, 40
SM_AW, SM_S, SM_N, SM_CV, SM_END = 0, 24, 120, 184, 312
NORMS = 3


def build_program(nc, x_prompt, x_sample, state_conv, state_c, state_n, state_m, g_ffn1, w_gu1, w_dn1,
                  g_mix, w_in, w_conv, b_i, b_f, g_head, w_pa, w_pb, w_out, g_ffn2, w_gu2, w_dn2, g_final,
                  y_prompt, y_sample, conv_p, c_p, n_p, m_p, conv_s, c_s, n_s, m_s):
    with ExitStack() as ctx:
        def sb(name, shape, dt=F32):
            return ctx.enter_context(nc.sbuf_tensor(name, shape, dt))

        def sem(name):
            return ctx.enter_context(nc.semaphore(name))

        X = sb("residual", [P, KT, T])
        A_h = sb("operand_hi", [P, KT, T], F32R)
        A_l = sb("operand_lo", [P, KT, T], F32R)
        wide = sb("wide_operand", [P, M_TILE + 2 * KT, T], F32R)
        G_h, G_l = wide[:, 0:FT, :], wide[:, FT:2 * FT, :]
        B_h, B_l = wide[:, 0:VT_TILES, :], wide[:, VT_TILES:2 * VT_TILES, :]
        M_h, M_l = wide[:, M_TILE:M_TILE + KT, :], wide[:, M_TILE + KT:M_TILE + 2 * KT, :]
        v_rows = wide[:, 2 * VT_TILES:2 * VT_TILES + 8, :].rearrange("p a t -> p (a t)")[:, 0:H * DV]
        QK = sb("q_k", [P, 2 * KT, T])
        GA, GM = QK[:, 0:KT, :], QK[:, KT:2 * KT, :]
        VH = sb("v_heads", [P, VT_TILES, T])
        k_tok = sb("k_tokens", [P, 2, H * DK])
        v_tok = sb("v_tokens", [P, 2, H * DV])
        U = sb("conv_input", [P, KT, T])
        C = [sb(f"c_state{i}", [P, KPH, DV]) for i in range(2)] + \
            [v_tok[:, i // 2, (i % 2) * KPH * DV:(i % 2 + 1) * KPH * DV].rearrange("p (a b) -> p a b", a=KPH) for i in range(4)]
        raw = [sb(f"raw_ring{i}", [P, CHUNK]) for i in range(SLOTS)]
        hi = [sb(f"hi_ring{i}", [P, CHUNK], F32R) for i in range(SLOTS)]
        lo = [sb(f"lo_ring{i}", [P, CHUNK], F32R) for i in range(SLOTS)]
        act_tmp = sb("act_tmp", [P, 2, T])
        val = sb("value_tmp", [P, 2, T])
        val2 = sb("value_tmp2", [P, 2, T])
        sq = sb("squares", [P, 2, T])
        sq_sum = sb("square_sums", [P, 2, T])
        rstd = sb("rstd", [P, T])
        stage = sb("stage", [P, 2, DV])
        ident = sb("identity", [P, P])
        ones = sb("ones", [P, P])
        causal = sb("causal_limit", [P, NP])
        eps = sb("eps", [P, 1])
        pick = sb("pick_sample", [P, NS], F32R)
        par = sb("parameters", [P, DEPTH * PARS + KT])
        bias_i = sb("bias_i", [H, DEPTH])
        bias_f = sb("bias_f", [H, DEPTH])
        wg = sb("gate_weights", [P, KT, 2 * H])
        wg_h, wg_l = (wide[:, WG_TILE + 2 * i:WG_TILE + 2 * i + 2, :].rearrange("p a t -> p (a t)")[:, 0:KT * 36 + P - 36] for i in range(2))
        rows = sb("head_rows", [H, 2, NP])
        s_rows = sb("sample_rows", [H, 3, NS])
        m_new = sb("m_new", [H, NS])
        m_old = sb("m_old", [H, NS])
        n_old = sb("n_old", [NS * H, DK])
        small = sb("small_transposed", [P, SM_END])
        q_s = sb("q_samples", [P, H, KPH, NS])
        wk_s = sb("wk_samples", [P, H, KPH, NS])
        n_new = sb("n_new", [P, KPH, H, NS])
        qn = sb("q_times_n", [P, KPH, H, NS])
        qn_sum = sb("q_n_sum", [P, H, NS])
        r_den = sb("sample_reciprocal", [P, H, NS])
        gate_s = sb("sample_gate", [P, VT_TILES, NS])
        h_sum = sb("sample_square_sum", [P, H, NS])
        u_keep = sb("conv_tail", [P, KT, 2 + NS])
        np_col = sb("n_prompt_columns", [P, H * KPH])
        head_den = sb("head_denominators", [P, 2, H])
        head_ms = sb("head_square_columns", [P, 2, H])
        head_f = sb("head_factors", [P, 2, H])

        ps = ctx.enter_context(nc.psum_tensor("psum", [P, 8, 512], F32))
        V_BANK, S_BANK, T_BANK = 4, 5, 6

        decay = sq[:, :, :].rearrange("p a t -> p (a t)")[:, 0:NP + P]
        score = val2[:, :, :].rearrange("p a t -> p (a t)")[:, 0:NP + P]
        diag = [t[:, :, :].rearrange("p a t -> p (a t)")[:, 0:4 * P].rearrange("p (s t) -> p s t", s=4) for t in (sq_sum, sq)]
        n_out = val[0:NS * H, 0, 0:DK]
        q_c = act_tmp[:, :, :].rearrange("p a t -> p (a t)")[:, 0:DV]
        np_row = val2[0:H * KPH, 1, T - P:T]
        h_s = val2[:, 0, 0:P].rearrange("p (h v b) -> p h v b", h=H, v=VPH)
        h_sq = val2[:, 1, 0:P].rearrange("p (h v b) -> p h v b", h=H, v=VPH)
        gate_f = U[0:H, 0, :]
        gate_mn = U[0:H, 1, :]
        gate_na = U[0:H, 2, :]
        gate_ex = U[0:H, 3, :]
        gate_ln = U[0:H, 4, :]
        gate_lf = U[0:H, 5, :]
        gate_b = U[0:H, 6, 0:NP]
        gate_mx = U[0:H, 7, 0:NP]
        gate_i = sq[0:H, 0, :]
        s_inter = sq[0:H, 1, 0:NS]
        conv_rows = VH[0:2 * NS, 0:4, :].rearrange("p a t -> p (a t)")[:, 0:D]
        aw = VH[0:H, 12:15, 0:NP]
        rstd_sq = sq_sum[:, 0:1, :]
        rstd_2 = rstd[:, :].rearrange("p (a t) -> p a t", a=1).broadcast_to([P, 2, T])
        aw_t = small[:, SM_AW:SM_S].rearrange("p (kind st h) -> p kind st h", kind=3, st=2)
        s_bc = small[:, SM_S:SM_N].rearrange("p (h kind b) -> p h kind b", h=H, kind=3)
        n_t = small[:, SM_N:SM_CV].rearrange("p (kt b h) -> p kt b h", kt=KPH, b=NS)
        cv_t = small[:, SM_CV:SM_END].rearrange("p (t b j) -> p t b j", t=KT, b=NS)
        x_rows = VH[:, 0:8, :].rearrange("p a t -> p (a t)")[:, 0:2 * D].rearrange("p (s d) -> p s d", s=2)
        xs_rows = VH[0:NS, 8:12, :].rearrange("p a t -> p (a t)")[:, 0:D]
        par_rows = k_tok[:, 0, 0:P]
        gf_rows = k_tok[0:KT, 1, 0:P]
        g_rows = QK[:, 0:4, :].rearrange("p a t -> p (a t)")[:, 0:D]
        y_banks = (T_BANK, 0, 2)
        y_rms = ps[:, S_BANK, 0:3]
        y_scale = head_f[:, :, :].rearrange("p a h -> p (a h)")[:, 0:3]
        y_rows = VH[:, 0:12, :].rearrange("p a t -> p (a t)")[:, 0:3 * D].rearrange("p (s d) -> p s d", s=3)

        pair = [ps[:, 0:2, 0:T], ps[:, 2:4, 0:T]]
        num_s = ps[:, S_BANK, 0:P].rearrange("p (h v b) -> p h v b", h=H, v=VPH)
        den_s = ps[:, S_BANK, P:P + H * NS]
        n_rows_ps = ps[0:NS * H, S_BANK, 256:512]
        den_c = ps[:, S_BANK, 160:168].rearrange("p (st h) -> p st h", st=2)
        ms_c = ps[:, S_BANK, 168:176].rearrange("p (st h) -> p st h", st=2)
        np_ps = ps[:, S_BANK, 176:176 + H * KPH]
        npt_ps = ps[0:H * KPH, S_BANK, 256:256 + P]

        w_loaded = [sem(f"w_loaded{i}") for i in range(SLOTS)]
        split_hi = sem("split_hi")
        split_lo = sem("split_lo")
        chunk_done = sem("chunk_done")
        pair_free = [sem("pair0_free"), sem("pair1_free")]
        const_ready = sem("const_ready")
        passed = sem("passed")
        prep_loaded = sem("prep_loaded")
        prep_tr = sem("prep_transposed")
        prep_copied = sem("prep_copied")
        small_loaded = sem("small_loaded")
        x_ready = sem("residual_ready")
        x_loaded = sem("inputs_loaded")
        block1_copied = sem("second_block_copied")
        g_loaded = sem("final_gains_loaded")
        sq_ready = sem("sq_ready")
        sums_ready = sem("sums_ready")
        norm_sum = sem("norm_sum")
        norm_root = sem("norm_root")
        operand_hi = sem("operand_hi_ready")
        operand_ready = sem("operand_ready")
        gate_done = sem("gate_done")
        hidden_hi = sem("hidden_hi")
        hidden_ready = sem("hidden_ready")
        wg_zero = sem("gate_weights_zero")
        wg_hi = sem("wg_hi")
        wg_ready = sem("wg_ready")
        gates_done = sem("gates_done")
        gate_exp_in = sem("gate_exp_in")
        gate_log = sem("gate_log")
        gate_rows = sem("gate_rows")
        gate_exps = sem("gate_exps")
        small_done = sem("small_done")
        small_copied = sem("small_copied")
        tr_done = sem("tokens_transposed")
        tr_free = [sem("tr_bank0_free"), sem("tr_bank1_free")]
        v_zero = sem("v_rows_zero")
        v_hi = sem("v_rows_hi")
        qn_ready = sem("qn_ready")
        den_done = sem("sample_den_done")
        n_out_ready = sem("n_out_ready")
        score_done = sem("score_done")
        decay_arg = sem("decay_arg")
        decay_ready = sem("decay_ready")
        score_ready = sem("score_ready")
        av_done = sem("av_done")
        av_read = sem("av_read")
        columns_done = sem("columns_done")
        columns_read = sem("columns_read")
        head_root = sem("head_root")
        diag_ready = sem("diag_ready")
        factors_done = sem("factors_done")
        cp_done = sem("c_prompt_done")
        cp_copied = sem("c_prompt_copied")
        np_done = sem("n_prompt_done")
        npt_done = sem("n_prompt_transposed")
        npt_copied = sem("n_prompt_rows_copied")
        tail_done = sem("tail_transposed")
        tail_copied = sem("tail_copied")
        c_loaded = [sem(f"c_loaded{i}") for i in range(6)]
        c_stored = [sem(f"c_stored{i}") for i in range(6)]
        vbc_done = sem("value_broadcast")
        c_scaled = sem("c_scaled")
        c_new = sem("c_new")
        q_c_ready = sem("q_times_c_ready")
        num_done = sem("sample_num_done")
        hs_sum_ready = sem("sample_sum_ready")
        hs_sum = sem("sample_sum_done")
        hs_root = sem("sample_root")
        ya_hi = sem("convolution_operand_hi")
        b_ready = sem("gated_heads_ready")
        y_tr = sem("y_transposed")
        y_sums = sem("y_sums")
        y_root = sem("y_root")
        y_copied = sem("y_copied")
        stored = sem("stored")
        m_stored = sem("m_stored")
        stage_stored = [sem("stage_stored0"), sem("stage_stored1")]
        n_stored = sem("n_stored")
        n_read = sem("n_stores_read")
        sig_done = sem("sigmoid_done")
        PER_SLOT = [7, 7, 5, 5, 4, 4]
        SMALL_LOADS = 5
        STAGE_STORES = H + 1
        PREP_LOADS = DEPTH * 5 + 3

        block = ctx.enter_context(nc.Block())

        def own_step(eng):
            eng.sem_inc(passed, 1)

        def par_loads(eng, l0, l1):
            for i in range(l0, l1):
                for off, n, src in ((PAR_FFN1, 8, g_ffn1[i]), (PAR_MIX, 8, g_mix[i]), (PAR_FFN2, 8, g_ffn2[i]),
                                    (PAR_CONV, 24, w_conv[i].rearrange("j d -> (j d)")), (PAR_HEAD, 16, g_head[i])):
                    at = i * PARS + off
                    eng.dma_start(par_rows[at:at + n, :], src.rearrange("(t p) -> t p", p=P)).then_inc(prep_loaded, 16)

        @block.sync
        def _(sp):
            def load(l, c, slot, dst, src):
                sp.wait_ge(split_lo, l * CHUNKS + c + 1)
                own_step(sp)
                sp.dma_start(dst, src).then_inc(w_loaded[slot], 16)

            def rows_of(w, l, k0, n, col):
                return w[bass.ds(l, 1), k0 * P:(k0 + n) * P, bass.ds(col, GW)].rearrange(
                    "a (k p) n -> p (a k) n", p=P)

            def to(slot, n=CK):
                return raw[slot][:, 0:n * GW].rearrange("p (k n) -> p k n", n=GW)

            def ffn(l, base, w_gu, w_dn):
                with sp.Fori(0, FFN_PAIRS) as i:
                    for j in range(4):
                        load(l, i * 4 + (base + j), j, to(j),
                             rows_of(w_gu, l, CK * (j % 2), CK, i * GW + (j // 2) * D_FF))
                with sp.Fori(0, DOWN_GROUPS // 2) as i:
                    for j in range(2 * DOWN_CHUNKS):
                        k0 = CK * (j % DOWN_CHUNKS)
                        n = min(CK, FT - k0)
                        load(l, i * (2 * DOWN_CHUNKS) + (base + C_DOWN + j), j % SLOTS, to(j % SLOTS, n),
                             rows_of(w_dn, l, k0, n, i * (2 * GW) + GW * (j // DOWN_CHUNKS)))

            def unit(l, c0, col):
                for j in range(8):
                    load(l, c0 + j, j % SLOTS, to(j % SLOTS), rows_of(w_in, l, CK * (j % 2), CK, col + GW * (j // 2)))

            par_loads(sp, 1, DEPTH)
            with sp.Fori(0, DEPTH) as l:
                ffn(l, 0, w_gu1, w_dn1)
                with sp.Fori(0, 4) as i:
                    unit(l, i * 8 + C_IN, i * D + U_Q * D)
                unit(l, C_IN + 32, U_GC * D)
                unit(l, C_IN + 40, U_XA * D)
                unit(l, C_IN + 48, U_GB * D)
                with sp.Fori(0, 2) as i:
                    unit(l, i * 8 + (C_IN + 56), i * D + U_O * D)
                with sp.Fori(0, 2) as i:
                    unit(l, i * 8 + (C_IN + 72), i * D + (GATE_COL + 2 * H))
                with sp.Fori(0, 2) as i:
                    for j in range(4):
                        load(l, i * 4 + (C_PA + j), j, to(j), rows_of(w_pa, l, CK * (j % 2), CK, i * (2 * GW) + GW * (j // 2)))
                with sp.Fori(0, 4) as i:
                    for j in range(4):
                        load(l, i * 4 + (C_PB + j), j, to(j), rows_of(w_pb, l, CK * j, CK, i * GW))
                with sp.Fori(0, 2) as i:
                    for j in range(4):
                        load(l, i * 4 + (C_WO + j), j, to(j), rows_of(w_out, l, CK * (j % 2), CK, i * (2 * GW) + GW * (j // 2)))
                ffn(l, C_FFN2, w_gu2, w_dn2)
            sp.wait_ge(chunk_done, 1 + (DEPTH - 1) * CHUNKS + C_FFN2)
            sp.dma_start(g_rows, g_final.rearrange("(a d) -> a d", a=1).broadcast_to([P, D])).then_inc(g_loaded, 16)

        @block.gpsimd
        def _(pool):
            pool.memset(ident[:, :], 0.0)
            pool.memset(causal[:, :], 0.0)
            pool.drain()
            pool.affine_select(out=ident[:, :], in_=ident[:, :], compare_op=ALU.not_equal, fill=1.0, base=0,
                               pattern=[[-1, P]], channel_multiplier=1)
            pool.affine_select(out=causal[:, :], in_=causal[:, :], compare_op=ALU.is_ge, fill=-1e30, base=0,
                               pattern=[[1, NP]], channel_multiplier=-1)
            pool.drain()
            pool.memset(eps[:, :], EPS).then_inc(const_ready, 1)

            for s in (x_ready, chunk_done, *pair_free, *tr_free, *c_stored, *stage_stored, n_stored, m_stored, c_new, b_ready):
                pool.sem_inc(s, 1)

            with pool.Fori(0, DEPTH) as l:
                pool.wait_ge(chunk_done, 1 + l * CHUNKS)
                own_step(pool)
                pool.memset(wg_h.bitcast(F32), 0.0)
                pool.memset(wg_l.bitcast(F32), 0.0).then_inc(wg_zero, 1)
                pool.wait_ge(chunk_done, 1 + l * CHUNKS + C_IN)
                own_step(pool)
                pool.memset(v_rows[:, :].bitcast(F32), 0.0).then_inc(v_zero, 1)

                def load_c(n, s, stores, b, h):
                    pool.wait_ge(num_done, l * (NS * H) + (n + (1 if s < 2 else -1)))
                    pool.wait_ge(c_stored[s], 1 + l * (16 * PER_SLOT[s]) + stores * 16)
                    pool.dma_start(C[s][:, :, :], state_c[bass.ds(l, 1), b, bass.ds(h, 1)].rearrange(
                        "x y (kt p) v -> p (x y kt) v", p=P)).then_inc(c_loaded[s], 16)

                for n in range(12):
                    load_c(n, n % 2, n // 2, 4 + n // H, n % H)
                pool.wait_ge(cp_copied, l * (2 * H) + 2 * H)
                own_step(pool)
                with pool.Fori(0, H) as h:
                    for b in range(4):
                        load_c(h * 4 + (12 + b), 2 + b, h, b, h)
                for h in range(H):
                    load_c(28 + h, h, PER_SLOT[h] - 1, NS - 1, h)

        def act_split(act, l, c, slot):
            act.wait_ge(w_loaded[slot], l * (16 * CHUNKS // SLOTS) + (c - slot) * 4 + 16)
            act.activation(hi[slot][:, :], raw[slot][:, :], ACT.Copy).then_inc(split_hi, 1)

        def dve_split(dve, l, c, slot):
            dve.wait_ge(split_hi, l * CHUNKS + c + 1)
            dve.tensor_tensor(lo[slot][:, :], raw[slot][:, :], hi[slot][:, :].bitcast(F32),
                              ALU.subtract).then_inc(split_lo, 1)

        def token_bank(t):
            return (T_BANK, T_BANK + 1, V_BANK, S_BANK)[t] if t < 4 else T_BANK + t % 2

        def token_dst(t):
            n, dst = (t - 4, k_tok) if t < 8 else (t - 8, v_tok)
            return dst[:, n % 2, (n // 2) * 512:(n // 2 + 1) * 512]

        def l1_states(i, j):
            return (i - 1 + j,) if i == 11 or (1 <= i < 11 and j == 0) else ()

        def state_chunk(i, g, n0):
            return 1 if n0 == 12 and i == 0 and g == 0 else 0

        @block.scalar
        def _(act):
            def ahead(l, c, j):
                act.wait_ge(chunk_done, 1 + l * CHUNKS + c)
                act_split(act, l, c + AHEAD, (j + AHEAD) % SLOTS)

            for s in range(2):
                act.dma_start(x_rows[:, s, :], x_prompt[0, s * P:(s + 1) * P, :]).then_inc(x_loaded, 16)
            act.dma_start(xs_rows, x_sample[:, 0, :]).then_inc(x_loaded, 16)
            par_loads(act, 0, 1)
            act.dma_start(gf_rows, g_final.rearrange("(t p) -> t p", p=P)).then_inc(prep_loaded, 16)
            act.dma_start(bias_i[:, :], b_i.rearrange("l h -> h l"), allow_slow_non_contiguous=True).then_inc(prep_loaded, 16)
            act.dma_start(bias_f[:, :], b_f.rearrange("l h -> h l"), allow_slow_non_contiguous=True).then_inc(prep_loaded, 16)

            norm_n = [0]

            def squares(l, q, ready=None):
                n = norm_n[0]
                norm_n[0] += 1
                if ready:
                    act.wait_ge(*ready)
                if q >= 2:
                    act.wait_ge(sums_ready, l * (3 * NORMS) + (n // 4 * 3 + q - 1))
                dst = sq if q else sq_sum
                act.activation(dst[:, :, :], X[:, 2 * q:2 * q + 2, :], ACT.Square).then_inc(sq_ready, 1)

            def operand_his(l, q, off, ready=None):
                if ready:
                    act.wait_ge(*ready)
                for f in range(2):
                    k = 2 * q + f
                    ins = act.activation(A_h[:, k, :], X[:, k, :], ACT.Copy, scale=par[:, bass.ds(l * PARS + (off + k), 1)])
                ins.then_inc(operand_hi, 1)

            def norm_root_of(l, n):
                act.wait_ge(norm_sum, l * NORMS + (n + 1))
                act.activation(rstd[:, :], ps[:, 7, 0:T], ACT.Sqrt, bias=eps[:, 0:1], scale=1.0 / D).then_inc(norm_root, 1)

            def ffn(l, which, c0, g0, norm, off):
                def pair_of(i, first):
                    for j in range(4):
                        ahead(l, i * 4 + (c0 + j), j)
                        if first and j == 1:
                            norm_root_of(l, norm)
                        if j == 2:
                            act.wait_ge(pair_free[0], 1 + l * (GROUPS // 2) + (i + (g0 // 2 + 1)))
                            act.activation(act_tmp[:, :, :], act_tmp[:, :, :], ACT.Silu).then_inc(gate_done, 1)
                    act.wait_ge(pair_free[1], 1 + l * (GROUPS // 2) + (i + (g0 // 2 + 1)))
                    act.activation(G_h[:, bass.ds(i * 2, 2), :], val[:, :, :], ACT.Copy).then_inc(hidden_hi, 1)

                pair_of(0, True)
                with act.Fori(1, FFN_PAIRS) as i:
                    pair_of(i, False)
                for g in range(DOWN_GROUPS):
                    for j in range(DOWN_CHUNKS):
                        c = c0 + C_DOWN + g * DOWN_CHUNKS + j
                        if c + AHEAD < CHUNKS:
                            ahead(l, c, c)
                    if which == 0 or g < 3:
                        operand_his(l, g, off, (x_ready, 1 + l * 8 + (which * 4 + g + 1)))
                        squares(l, g)

            act.wait_ge(const_ready, 1)
            act.wait_ge(prep_tr, 2)
            for half in range(2):
                ins = act.activation(X[:, 4 * half:4 * half + 4, P:2 * P],
                                     ps[:, 2 + half, :].rearrange("p (k t) -> p k t", k=4), ACT.Copy)
            ins.then_inc(block1_copied, 1)
            act.wait_ge(block1_copied, 1)
            act.wait_ge(prep_copied, 3)
            for q in range(3):
                squares(0, q)
                if q == 0:
                    act.wait_ge(prep_copied, 4)
                operand_his(0, q, PAR_FFN1)

            with act.Fori(0, DEPTH) as l:
                def l1(c=0):
                    return l + (1 + c)

                act.wait_ge(chunk_done, 1 + l * CHUNKS)
                own_step(act)
                act_split(act, l, 0, 0)
                norm_n[0] = 3
                operand_his(l, 3, PAR_FFN1, (x_ready, 1 + l * 8))
                squares(l, 3)
                for c in range(1, AHEAD):
                    act_split(act, l, c, c)
                act.dma_start(n_old[:, :], state_n[bass.ds(l, 1)].rearrange("a b h k -> (a b h) k")).then_inc(small_loaded, 16)
                act.dma_start(m_old[:, :], state_m[bass.ds(l, 1)].rearrange("a b h -> h (a b)"), allow_slow_non_contiguous=True).then_inc(small_loaded, 16)
                act.wait_ge(prep_tr, 4)
                act.dma_start(conv_rows, state_conv[bass.ds(l, 1)].rearrange("a b j d -> (a b j) d")).then_inc(small_loaded, 16)
                act.dma_start(wg[:, :, :], w_in[bass.ds(l, 1), :, GATE_COL:GATE_COL + 2 * H].rearrange(
                    "a (k p) n -> p (a k) n", p=P)).then_inc(small_loaded, 16)
                act.dma_start(conv_s[bass.ds(l, 1), :, 0, :], state_conv[bass.ds(l, 1), :, 1, :]).then_inc(small_loaded, 16)

                ffn(l, 0, 0, 0, 0, PAR_MIX)

                def unit(c0, evac, sample=lambda g, s: None, last=lambda g: None):
                    for g in range(4):
                        for j in range(2):
                            sample(g, j)
                            ahead(l, c0 + 2 * g + j, 2 * g + j)
                        if evac:
                            evac(g)
                        last(g)

                def gate_weights(g):
                    if g == 0:
                        norm_root_of(l, 1)
                    if g == 1:
                        act.wait_ge(wg_zero, l1())
                        act.wait_ge(small_loaded, l * (16 * SMALL_LOADS) + 16 * SMALL_LOADS)
                        for part, w0 in enumerate((0, 32)):
                            ins = act.activation(wg_h[:, 0:KT * 36].rearrange("p (k c) -> p k c", c=36)[:, :, w0:w0 + H],
                                                 wg[:, :, part * H:part * H + H], ACT.Copy)
                        ins.then_inc(wg_hi, 1)

                def gate_part(g):
                    if g == 0:
                        act.wait_ge(gate_exp_in, l1())
                        act.activation(gate_ex, gate_na, ACT.Exp)
                        act.drain()
                        act.activation(gate_ln, gate_ex, ACT.Ln, bias=ones[0:H, 0:1]).then_inc(gate_log, 1)
                    if g == 2:
                        act.wait_ge(gate_rows, l1())
                        act.activation(aw[:, 1, :], aw[:, 0, :], ACT.Exp, bias=rows[:, 0, NP - 1:NP])
                        act.activation(aw[:, 2, :], rows[:, 1, :], ACT.Exp, scale=-1.0)
                        act.activation(s_rows[:, :, :], s_rows[:, :, :], ACT.Exp).then_inc(gate_exps, 1)
                        act.dma_start(m_p[bass.ds(l, 1), 0, :].rearrange("a h -> h a"), rows[:, 1, NP - 1:NP],
                                      allow_slow_non_contiguous=True).then_inc(m_stored, 16)
                        act.dma_start(m_s[bass.ds(l, 1)].rearrange("a b h -> h (a b)"), m_new[:, :],
                                      allow_slow_non_contiguous=True).then_inc(m_stored, 16)

                unit(C_IN, None, last=gate_weights)
                unit(C_IN + 8, None, last=gate_part)
                with act.Fori(0, 2) as i:
                    unit(i * 8 + (C_IN + 16), None)

                def scale_c(n, s, stores, b, h):
                    act.wait_ge(c_loaded[s], l * (16 * PER_SLOT[s]) + (stores * 16 + 16))
                    act.activation(C[s][:, :, :], C[s][:, :, :], ACT.Copy,
                                   scale=s_bc[:, bass.ds(h, 1), 0, b:b + 1].rearrange("p a c -> p (a c)")).then_inc(c_scaled, 1)

                def store_c(n, s, b, h):
                    act.wait_ge(c_new, 1 + l * (NS * H) + (n + 1))
                    act.dma_start(c_s[bass.ds(l, 1), b, bass.ds(h, 1)].rearrange("x y (kt p) v -> p (x y kt) v", p=P),
                                  C[s][:, :, :]).then_inc(c_stored[s], 16)

                def samples(i, n0):
                    h = i + (n0 - 12) // 4
                    def step(g, j):
                        if j == state_chunk(i, g, n0):
                            scale_c(i * 4 + (n0 + g), 2 + g, h, g, h)
                    return step, lambda g: store_c(i * 4 + (n0 + g), 2 + g, g, h)

                def token_copy(t):
                    act.wait_ge(tr_done, l * 16 + (t + 1))
                    act.activation(token_dst(t), ps[:, T_BANK + t % 2, :], ACT.Copy).then_inc(tr_free[t % 2], 1)

                def v_row_hi(t):
                    act.wait_ge(v_zero, l1())
                    act.wait_ge(tr_done, l * 16 + (t + 1))
                    act.activation(v_rows[0:NS, t * 512:(t + 1) * 512], ps[0:NS, token_bank(t), :],
                                   ACT.Copy).then_inc(v_hi, 1)

                def head_exps(h):
                    act.wait_ge(decay_arg, l * H + (h + 1))
                    act.activation(decay, decay, ACT.Exp).then_inc(decay_ready, 1)

                def head_square(h):
                    act.wait_ge(av_done, l * H + (h + 1))
                    both = ps[:, T_BANK:T_BANK + 2, :].rearrange("p a (b t) -> p (a b) t", b=2)
                    for s in range(2):
                        act.wait_ge(stage_stored[s], 1 + l * (16 * STAGE_STORES) + 16 * h)
                    act.activation(stage[:, :, :].rearrange("p a (b t) -> p (a b) t", b=2), both, ACT.Square)
                    act.activation(VH[:, VPH * h:VPH * h + VPH, 0:NP], both, ACT.Copy).then_inc(av_read, 1)

                def prompt_state(h):
                    for s in range(KPH):
                        act.wait_ge(cp_done, l * (2 * H) + (2 * h + s + 1))
                        act.activation(stage[:, s, :], ps[:, T_BANK + s, :], ACT.Copy).then_inc(cp_copied, 1)
                    for s in range(KPH):
                        act.wait_ge(cp_copied, l * (2 * H) + (2 * h + s + 1))
                        act.dma_start(c_p[bass.ds(l, 1), 0, h, s * P:(s + 1) * P, :].rearrange("a p v -> p (a v)"),
                                      stage[:, s, :]).then_inc(stage_stored[s], 16)

                def l1_state(i, j):
                    for n in l1_states(i, j):
                        scale_c(n, n % 2, n // 2, 4 + n // H, n % H)

                def l1_last(i):
                    for j in range(2):
                        for n in l1_states(i, j):
                            store_c(n, n % 2, 4 + n // H, n % H)
                    if i == 0:
                        for t in range(4):
                            v_row_hi(t)
                    l1_state(i + 1, 0)
                    if 1 <= i < 4:
                        for t in range(4 * i, 4 * i + 4):
                            token_copy(t)
                    if i >= 5 and i % 2 == 1:
                        prompt_state((i - 5) // 2)
                    if i >= 3 and i % 2 == 1 and i < 11:
                        head_exps((i - 3) // 2)
                    if i >= 4 and i % 2 == 0:
                        head_square((i - 4) // 2)

                unit(C_IN + 32, None, last=l1_last)
                act.wait_ge(n_out_ready, l1())
                for h in range(H):
                    act.dma_start(n_s[bass.ds(l, 1), :, h, :].rearrange("a b k -> (a b) k"),
                                  n_out[h * NS:(h + 1) * NS, :]).then_inc(n_stored, 16)
                unit(C_IN + 40, None, last=lambda g: l1_last(4 + g))
                act.wait_ge(n_stored, 1 + l * (16 * (H + 1)) + 16 * H)
                act.sem_inc(n_read, 1)
                unit(C_IN + 48, None, lambda g, j: l1_state(8 + g, 1) if j else None, lambda g: l1_last(8 + g))

                act.wait_ge(columns_read, l1())
                act.activation(head_ms[:, :, :], head_ms[:, :, :], ACT.Sqrt, bias=eps[:, 0:1], scale=1.0 / DV).then_inc(head_root, 1)
                act.wait_ge(tail_copied, l1())
                act.dma_start(conv_p[bass.ds(l, 1), 0].rearrange("a r d -> (a r) d"),
                              stage[0:2, :, :].rearrange("p a b -> p (a b)")).then_inc(stage_stored[0], 16)
                act.dma_start(conv_s[bass.ds(l, 1), :, 1, :].rearrange("a b d -> (a b) d"),
                              stage[2:2 + NS, :, :].rearrange("p a b -> p (a b)")).then_inc(stage_stored[1], 16)


                def sigmoids(i, g, name, t):
                    act.wait_ge(pair_free[g % 2], 1 + l * (GROUPS // 2) + (i * 2 + (ORDER_G[name] // 2 + g // 2 + 1)))
                    act.activation(t, t, ACT.Sigmoid).then_inc(sig_done, 1)

                for i in range(2):
                    unit(i * 8 + (C_IN + 56), lambda g: sigmoids(i, g, "o0", act_tmp[:, :, :]), *samples(i, 12))
                act.wait_ge(npt_copied, l1())
                act.dma_start(n_p[bass.ds(l, 1), 0].rearrange("a h (kt p) -> (a h kt) p", p=P), np_row).then_inc(n_stored, 16)
                with act.Fori(0, 2) as i:
                    unit(i * 8 + (C_IN + 72), lambda g: sigmoids(i, g, "ga", QK[:, bass.ds(i * 8 + 2 * g, 2), :]), *samples(i, 20))

                act.wait_ge(chunk_done, 1 + l * CHUNKS + C_PA)
                own_step(act)
                for q in range(4):
                    act.activation(A_h[:, 2 * q:2 * q + 2, :], U[:, 2 * q:2 * q + 2, :], ACT.Copy).then_inc(ya_hi, 1)
                for g in range(4):
                    for j in range(2):
                        if g < 2:
                            h = 2 * g + j
                            scale_c(28 + h, h, PER_SLOT[h] - 1, NS - 1, h)
                        ahead(l, C_PA + 2 * g + j, 2 * g + j)
                    for h in (2 * g, 2 * g + 1) if g < 2 else ():
                        store_c(28 + h, h, NS - 1, h)
                    if g == 2:
                        act.wait_ge(hs_sum, l1())
                        act.activation(r_den[:, :, :], den_s, ACT.Sqrt, bias=eps[:, 0:1], scale=1.0 / DV).then_inc(hs_root, 1)
                with act.Fori(0, 4) as i:
                    for j in range(4):
                        ahead(l, i * 4 + (C_PB + j), j)
                for g in range(4):
                    for j in range(2):
                        ahead(l, C_WO + 2 * g + j, 2 * g + j)
                    operand_his(l, g, PAR_FFN2, (pair_free[g % 2], 1 + l * (GROUPS // 2) + (G_WO // 2 + g // 2 + 1)))
                    squares(l, g)
                ffn(l, 1, C_FFN2, G_FFN2, 2, PARS + PAR_FFN1)

            norm_n[0] = 3
            squares(DEPTH, 3, (x_ready, 1 + DEPTH * 8))
            act.wait_ge(y_sums, 1)
            act.activation(y_scale[:, 0:2], y_rms[:, 0:2], ACT.Sqrt, bias=eps[:, 0:1], scale=1.0 / D)
            act.activation(y_scale[0:NS, 2:3], y_rms[0:NS, 2:3], ACT.Sqrt, bias=eps[0:NS, 0:1], scale=1.0 / D).then_inc(y_root, 1)
            for s in range(3):
                act.wait_ge(y_copied, 2 * (s + 1))
                dst, n = ((y_prompt[0, 0:P, :], P), (y_prompt[0, P:2 * P, :], P), (y_sample[:, 0, :], NS))[s]
                act.dma_start(dst, y_rows[0:n, s, :]).then_inc(stored, 16)
            act.wait_ge(stored, 16 * 3)
            act.wait_ge(small_loaded, DEPTH * 16 * SMALL_LOADS)
            act.wait_ge(m_stored, 1 + DEPTH * 16 * 2)
            for s in range(2):
                act.wait_ge(stage_stored[s], 1 + DEPTH * 16 * STAGE_STORES)
            act.wait_ge(n_stored, 1 + DEPTH * 16 * (H + 1))
            for s in range(6):
                act.wait_ge(c_stored[s], 1 + DEPTH * 16 * PER_SLOT[s])

        @block.vector
        def _(dve):
            TT, STT, TS = dve.tensor_tensor, dve.scalar_tensor_tensor, dve.tensor_scalar
            norm_n = [0]

            def ahead(l, c, j):
                dve_split(dve, l, c + AHEAD, (j + AHEAD) % SLOTS)

            def wait_group(l, c_end):
                dve.wait_ge(chunk_done, 1 + l * CHUNKS + c_end)

            def add_squares(l, q):
                n = norm_n[0]
                norm_n[0] += 1
                dve.wait_ge(sq_ready, l * (4 * NORMS) + (n + 1))
                if q:
                    if q > 1:
                        dve.wait_ge(sums_ready, l * (3 * NORMS) + (n // 4 * 3 + q - 1))
                    ins = TT(sq_sum[:, :, :], sq_sum[:, :, :], sq[:, :, :], ALU.add)
                    if q == 3:
                        dve.drain()
                        ins = TT(sq_sum[:, 0, :], sq_sum[:, 0, :], sq_sum[:, 1, :], ALU.add)
                    ins.then_inc(sums_ready, 1)

            def operand_los(l, q, off):
                dve.wait_ge(operand_hi, l * (4 * NORMS) + (norm_n[0] + 1))
                for f in range(2):
                    k = 2 * q + f
                    ins = STT(A_l[:, k, :], X[:, k, :], par_at(l, off + k), A_h[:, k, :].bitcast(F32), ALU.mult, ALU.subtract)
                ins.then_inc(operand_ready, 2)

            def norm_reciprocal(l, n):
                dve.wait_ge(norm_root, l * NORMS + (n + 1))
                dve.reciprocal(rstd[:, :], rstd[:, :])
                dve.drain()

            def par_at(l, c):
                return par[:, bass.ds(l * PARS + c, 1)]

            def ffn(l, which, c0, g0, norm, off):
                def pair_of(i, first):
                    at = l * (2 * FFN_PAIRS) + (i + (which * FFN_PAIRS + 1))
                    for j in range(4):
                        if j == 2:
                            wait_group(l, i * 4 + (c0 + 2))
                            TT(act_tmp[:, :, :], pair[0], rstd_2, ALU.mult).then_inc(pair_free[0], 1)
                        ahead(l, i * 4 + (c0 + j), j)
                        if first and j == 1:
                            norm_reciprocal(l, norm)
                    wait_group(l, i * 4 + (c0 + 4))
                    dve.wait_ge(gate_done, at)
                    TT(val[:, :, :], act_tmp[:, :, :], pair[1], ALU.mult).then_inc(pair_free[1], 1)
                    dve.wait_ge(hidden_hi, at)
                    TT(G_l[:, bass.ds(i * 2, 2), :], val[:, :, :], G_h[:, bass.ds(i * 2, 2), :].bitcast(F32),
                       ALU.subtract).then_inc(hidden_ready, 1)

                pair_of(0, True)
                with dve.Fori(1, FFN_PAIRS) as i:
                    pair_of(i, False)
                for g in range(DOWN_GROUPS):
                    for j in range(DOWN_CHUNKS):
                        c = c0 + C_DOWN + g * DOWN_CHUNKS + j
                        if c + AHEAD < CHUNKS:
                            ahead(l, c, c)
                    wait_group(l, c0 + C_DOWN + (g + 1) * DOWN_CHUNKS)
                    TT(val[:, :, :], pair[g % 2], rstd_2, ALU.mult).then_inc(pair_free[g % 2], 1)
                    dve.drain()
                    x = X[:, 2 * g:2 * g + 2, :]
                    STT(x, val[:, :, :], 0.5, x, ALU.mult, ALU.add).then_inc(x_ready, 1)
                    if which == 0 or g < 3:
                        operand_los(l, g, off)
                        add_squares(l, g)

            dve.memset(ones[:, :], 1.0).then_inc(split_lo, SLOTS)
            dve.wait_ge(const_ready, 1)
            TT(pick[:, :], ident[:, 0:NS], ident[:, 32:32 + NS], ALU.add).then_inc(prep_copied, 1)
            for s in (0, 2):
                dve.wait_ge(prep_tr, s + 1)
                n = P if s < 2 else NS
                for half in range(2):
                    ins = dve.tensor_copy(X[:, 4 * half:4 * half + 4, s * P:s * P + n],
                                          ps[:, (0, 2, T_BANK)[s] + half, 0:4 * n].rearrange("p (k t) -> p k t", k=4))
                ins.then_inc(prep_copied, 1)
            dve.wait_ge(prep_tr, 4)
            dve.tensor_copy(par[:, :], ps[:, 4, 0:DEPTH * PARS + KT]).then_inc(prep_copied, 1)
            dve.wait_ge(block1_copied, 1)
            dve.drain()
            for q in range(3):
                operand_los(0, q, PAR_FFN1)
                add_squares(0, q)

            with dve.Fori(0, DEPTH) as l:
                def l1(c=0):
                    return l + (1 + c)

                dve_split(dve, l, 0, 0)
                norm_n[0] = 3
                operand_los(l, 3, PAR_FFN1)
                add_squares(l, 3)
                for c in range(1, AHEAD):
                    dve_split(dve, l, c, c)
                ffn(l, 0, 0, 0, 0, PAR_MIX)

                def unit(c0, evac, sample=lambda g, s: None, last=lambda g: None):
                    for g in range(4):
                        for j in range(2):
                            sample(g, j)
                            ahead(l, c0 + 2 * g + j, 2 * g + j)
                        if evac:
                            wait_group(l, c0 + 2 * g + 2)
                            evac(g)
                        last(g)

                def scaled(dst):
                    def evac(g):
                        TT(dst(g), pair[g % 2], rstd_2, ALU.mult).then_inc(pair_free[g % 2], 1)
                    return evac

                def gate_part(g):
                    if g == -1:
                        dve.wait_ge(gates_done, l1())
                        TT(gate_i, ps[0:H, T_BANK, 0:T], rstd[0:H, :], ALU.mult)
                        TT(gate_f, ps[32:32 + H, T_BANK, 0:T], rstd[32:32 + H, :], ALU.mult)
                        dve.drain()
                        TS(gate_i, gate_i, bias_i[:, bass.ds(l, 1)], None, ALU.add)
                        TS(gate_f, gate_f, bias_f[:, bass.ds(l, 1)], None, ALU.add)
                        dve.drain()
                        TS(gate_mn, gate_f, 0.0, None, ALU.min)
                        dve.drain()
                        STT(gate_na, gate_mn, 2.0, gate_f, ALU.mult, ALU.subtract).then_inc(gate_exp_in, 1)
                    if g == 1:
                        dve.wait_ge(gate_log, l1())
                        TT(gate_lf, gate_mn, gate_ln, ALU.subtract)
                        dve.drain()
                        dve.tensor_tensor_scan(gate_b, ones[0:H, 0:1].broadcast_to([H, NP]), gate_lf[:, 0:NP], 0.0, ALU.mult, ALU.add)
                        dve.drain()
                        TT(aw[:, 0, :], gate_i[:, 0:NP], gate_b, ALU.subtract)
                        dve.drain()
                    if g == 2:
                        dve.tensor_tensor_scan(gate_mx, aw[:, 0, :], aw[:, 0, :], 0.0, ALU.max, ALU.max)
                        TT(s_inter, gate_lf[:, NP:T], m_old[:, :], ALU.add)
                        dve.drain()
                        dve.wait_ge(m_stored, 1 + l * 32)
                        TS(rows[:, 0, :], gate_mx, -1.0, None, ALU.mult)
                        TT(rows[:, 1, :], gate_b, gate_mx, ALU.add)
                        TT(m_new[:, :], s_inter, gate_i[:, NP:T], ALU.max)
                        dve.drain()
                        TT(s_rows[:, 0, :], s_inter, m_new[:, :], ALU.subtract)
                        TT(s_rows[:, 1, :], gate_i[:, NP:T], m_new[:, :], ALU.subtract)
                        TS(s_rows[:, 2, :], m_new[:, :], -1.0, None, ALU.mult).then_inc(gate_rows, 1)

                def q_evac(g):
                    if g == 0:
                        norm_reciprocal(l, 1)
                        rs = rstd[:, :].rearrange("p (a t) -> p a t", a=1)
                        TT(rstd_sq, rs, rs, ALU.mult)
                    scaled(lambda g: QK[:, 2 * g:2 * g + 2, :])(g)

                def gate_weights(g):
                    if g == 1:
                        dve.wait_ge(wg_hi, l1())
                        for part, w0 in enumerate((0, 32)):
                            at = [t[:, 0:KT * 36].rearrange("p (k c) -> p k c", c=36)[:, :, w0:w0 + H] for t in (wg_l, wg_h)]
                            ins = TT(at[0], wg[:, :, part * H:part * H + H], at[1].bitcast(F32), ALU.subtract)
                        ins.then_inc(wg_ready, 1)

                unit(C_IN, q_evac, last=gate_weights)
                unit(C_IN + 8, scaled(lambda g: QK[:, 8 + 2 * g:10 + 2 * g, :]),
                     lambda g, j: gate_part(-1) if (g, j) == (0, 1) else None, gate_part)
                dve.wait_ge(small_done, l1())
                dve.tensor_copy(small[:, :], ps[:, T_BANK, 0:SM_END]).then_inc(small_copied, 1)
                dve.drain()
                for p in range(2):
                    dve.wait_ge(pair_free[p], 1 + l * (GROUPS // 2) + (ORDER_G["v0"] // 2))
                TS(q_s[:, :, :, :].rearrange("p h k b -> p (h k) b"), QK[:, 0:KT, NP:T], DK ** -0.5, None, ALU.mult)
                for kt in range(KPH):
                    TT(wk_s[:, :, kt, :], QK[:, KT + kt:2 * KT:KPH, NP:T], s_bc[:, :, 1, :], ALU.mult)
                    TT(n_new[:, kt, :, :], n_t[:, kt, :, :].rearrange("p b h -> p h b"), s_bc[:, :, 0, :], ALU.mult)
                dve.drain()
                for kt in range(KPH):
                    TT(n_new[:, kt, :, :], n_new[:, kt, :, :], wk_s[:, :, kt, :], ALU.add)
                dve.drain()
                for kt in range(KPH):
                    TT(qn[:, kt, :, :], n_new[:, kt, :, :], q_s[:, :, kt, :], ALU.mult)
                dve.drain()
                TT(qn_sum[:, :, :], qn[:, 0, :, :], qn[:, 1, :, :], ALU.add).then_inc(qn_ready, 1)
                with dve.Fori(0, 2) as i:
                    unit(i * 8 + (C_IN + 16), scaled(lambda g: VH[:, bass.ds(i * 8 + 2 * g, 2), :]))

                def sample_state(n, s, b, h):
                    dve.wait_ge(c_scaled, l * (NS * H) + (n + 1))
                    dve.wait_ge(vbc_done, l * (NS * H) + (n + 1))
                    for kt in range(KPH):
                        w = wk_s[:, bass.ds(h, 1), kt, b:b + 1].rearrange("p a c -> p (a c)")
                        ins = STT(C[s][:, kt, :], ps[:, V_BANK, :], w, C[s][:, kt, :], ALU.mult, ALU.add)
                    ins.then_inc(c_new, 1)

                def state_sum(n, s, b, h):
                    dve.wait_ge(num_done, l * (NS * H) + (n + 2))
                    dve.wait_ge(c_new, 1 + l * (NS * H) + (n + 1))
                    q = [q_s[:, bass.ds(h, 1), kt, b:b + 1].rearrange("p a c -> p (a c)") for kt in range(KPH)]
                    TS(q_c, C[s][:, 0, :], q[0], None, ALU.mult)
                    dve.drain()
                    STT(q_c, C[s][:, 1, :], q[1], q_c, ALU.mult, ALU.add).then_inc(q_c_ready, 1)

                def samples(i, n0):
                    return lambda g, j: sample_state(i * 4 + (n0 + g), 2 + g, g, i + (n0 - 12) // 4) if j == state_chunk(i, g, n0) else None

                def l1_state(i, j):
                    for n in l1_states(i, j):
                        sample_state(n, n % 2, 4 + n // H, n % H)
                    if i >= 4 and i % 2 == 0 and j == 0:
                        head_score((i - 4) // 2)
                    for n in l1_states(i, 0) if j else ():
                        if n < SUMMED:
                            state_sum(n, n % 2, 4 + n // H, n % H)

                def v_row_lo(t):
                    dve.wait_ge(v_hi, l * 4 + (t + 1))
                    cols = slice(t * 512, (t + 1) * 512)
                    TT(v_rows[32:32 + NS, cols], ps[0:NS, token_bank(t), :], v_rows[0:NS, cols].bitcast(F32),
                       ALU.subtract).then_inc(tr_free[t % 2], 1)

                def head_decay(h):
                    dve.wait_ge(score_done, l * H + (h + 1))
                    STT(decay[:, 0:NP], ps[:, T_BANK + 1, 0:NP], aw_t[:, 0, 0, h:h + 1], causal[:, :], ALU.add, ALU.min)
                    STT(decay[:, NP:NP + P], ps[:, T_BANK + 1, P:NP], aw_t[:, 0, 1, h:h + 1], causal[:, 0:P],
                        ALU.add, ALU.min).then_inc(decay_arg, 1)
                    for st in range(2):
                        kk = k_tok[:, st, h * DK:(h + 1) * DK]
                        TS(kk, kk, aw_t[:, 1, st, h:h + 1], None, ALU.mult)

                def head_score(h):
                    dve.wait_ge(decay_ready, l * H + (h + 1))
                    STT(score, ps[:, T_BANK, 0:NP + P], DK ** -0.5, decay, ALU.mult, ALU.mult).then_inc(score_ready, 1)

                def head_factors():
                    dve.wait_ge(columns_done, l * H + H)
                    TT(head_den[:, :, :], den_c, aw_t[:, 2, :, :], ALU.max)
                    dve.tensor_copy(head_ms[:, :, :], ms_c)
                    dve.drain()
                    STT(head_den[:, :, :], den_c, -1.0, head_den[:, :, :], ALU.mult, ALU.max)
                    dve.drain()
                    dve.reciprocal(head_den[:, :, :], head_den[:, :, :])
                    dve.drain()
                    TT(head_ms[:, :, :], head_ms[:, :, :], head_den[:, :, :], ALU.mult)
                    dve.drain()
                    TT(head_ms[:, :, :], head_ms[:, :, :], head_den[:, :, :], ALU.mult).then_inc(columns_read, 1)

                def head_diagonals():
                    dve.wait_ge(head_root, l1())
                    dve.reciprocal(head_f[:, :, :], head_ms[:, :, :])
                    dve.drain()
                    TT(head_f[:, :, :], head_f[:, :, :], head_den[:, :, :], ALU.mult)
                    dve.drain()
                    for half in range(2):
                        for x in range(4):
                            ins = TS(diag[half][:, x, :], ident[:, :], head_f[:, x % 2, 2 * half + x // 2:2 * half + x // 2 + 1], None, ALU.mult)
                        ins.then_inc(diag_ready, 1)

                def sample_den():
                    dve.wait_ge(den_done, l1())
                    d = den_s.rearrange("p (h b) -> p h b", h=H)
                    TT(r_den[:, :, :], d, s_bc[:, :, 2, :], ALU.max)
                    dve.drain()
                    STT(r_den[:, :, :], d, -1.0, r_den[:, :, :], ALU.mult, ALU.max)
                    dve.drain()
                    dve.reciprocal(r_den[:, :, :], r_den[:, :, :])
                    dve.wait_ge(n_stored, 1 + l * (16 * (H + 1)))
                    dve.tensor_copy(n_out, n_rows_ps).then_inc(n_out_ready, 1)

                def l1_last(i):
                    if i == 0:
                        for t in range(4):
                            v_row_lo(t)
                        sample_den()
                    if i >= 3 and i % 2 == 1 and i < 11:
                        head_decay((i - 3) // 2)

                def xa_evac(g):
                    TT(U[:, 2 * g:2 * g + 2, :], U[:, 2 * g:2 * g + 2, :], pair[g % 2], ALU.mult).then_inc(pair_free[g % 2], 1)
                    dve.drain()
                    dve.tensor_copy(u_keep[:, 2 * g:2 * g + 2, :], U[:, 2 * g:2 * g + 2, NP - 2:T])

                def gb_evac(g):
                    for f in range(2):
                        k = 2 * g + f
                        w = [par_at(l, PAR_CONV + KT * j + k) for j in range(3)]
                        TS(val[:, f, :], U[:, k, :], w[2], None, ALU.mult)
                    for j in (1, 0):
                        dve.drain()
                        for f in range(2):
                            k = 2 * g + f
                            w = par_at(l, PAR_CONV + KT * j + k)
                            t = val[:, f, 2 - j:NP]
                            STT(t, U[:, k, 0:NP - 2 + j], w, t, ALU.mult, ALU.add)
                            t = val[:, f, NP:T]
                            STT(t, cv_t[:, k, :, j], w, t, ALU.mult, ALU.add)
                    dve.drain()
                    TT(val[:, :, :], val[:, :, :], rstd_2, ALU.mult)
                    dve.drain()
                    TT(U[:, 2 * g:2 * g + 2, :], val[:, :, :], pair[g % 2], ALU.mult).then_inc(pair_free[g % 2], 1)
                    dve.drain()

                def gc_evac(g):
                    TT(U[:, 2 * g:2 * g + 2, :], pair[g % 2], rstd_sq.broadcast_to([P, 2, T]), ALU.mult).then_inc(pair_free[g % 2], 1)

                unit(C_IN + 32, gc_evac, l1_state, l1_last)
                unit(C_IN + 40, xa_evac, lambda g, j: l1_state(4 + g, j), lambda g: l1_last(4 + g))
                dve.wait_ge(n_read, l1())
                own_step(dve)
                unit(C_IN + 48, gb_evac, lambda g, j: l1_state(8 + g, j), lambda g: l1_last(8 + g))

                dve.wait_ge(np_done, l * H + H)
                dve.wait_ge(num_done, l * (NS * H) + (12 + 2))
                dve.tensor_copy(np_col[:, :], np_ps)
                head_factors()
                dve.wait_ge(tail_done, l1())
                for s in range(2):
                    dve.wait_ge(stage_stored[s], 1 + l * (16 * STAGE_STORES) + 16 * H)
                dve.tensor_copy(stage[0:2 + NS, :, :], ps[0:2 + NS, T_BANK:T_BANK + 2, :]).then_inc(tail_copied, 1)
                head_diagonals()

                for i in range(2):
                    def o_evac(g):
                        tile = i * 8 + 2 * g
                        heads = VH[:, tile:tile + 2, 0:NP]
                        if tile == 0:
                            dve.wait_ge(npt_done, l1())
                            dve.tensor_copy(np_row, npt_ps).then_inc(npt_copied, 1)
                            dve.wait_ge(factors_done, l * 2 + 2)
                        TT(heads, heads, ps[:, T_BANK + i:T_BANK + i + 1, (g // 2) * NP:(g // 2 + 1) * NP].broadcast_to([P, 2, NP]), ALU.mult)
                        TT(act_tmp[:, :, :], pair[g % 2], rstd_2, ALU.mult).then_inc(pair_free[g % 2], 1)
                        dve.wait_ge(sig_done, l * 16 + (i * 4 + (g + 1)))
                        for f in range(2):
                            w = par[:, bass.ds(l * PARS + (i * 8 + (PAR_HEAD + 2 * g + f)), 1)]
                            STT(val[:, f, 0:NP], act_tmp[:, f, 0:NP], w,
                                VH[:, bass.ds(tile + f, 1), 0:NP].rearrange("p a t -> p (a t)"), ALU.mult, ALU.mult)
                            TS(gate_s[:, bass.ds(tile + f, 1), :].rearrange("p a b -> p (a b)"), act_tmp[:, f, NP:T], w, None, ALU.mult)
                        dve.drain()
                        dve.tensor_copy(B_h[:, bass.ds(tile, 2), 0:NP], val[:, :, 0:NP])
                        dve.drain()
                        TT(B_l[:, bass.ds(tile, 2), 0:NP], val[:, :, 0:NP], B_h[:, bass.ds(tile, 2), 0:NP].bitcast(F32),
                           ALU.subtract).then_inc(b_ready, 1)
                    unit(i * 8 + (C_IN + 56), o_evac, samples(i, 12))
                with dve.Fori(0, 2) as i:
                    unit(i * 8 + (C_IN + 72), scaled(lambda g: QK[:, bass.ds(i * 8 + 2 * g, 2), :]), samples(i, 20))

                for q in range(4):
                    dve.wait_ge(ya_hi, l * 4 + (q + 1))
                    TT(A_l[:, 2 * q:2 * q + 2, :], U[:, 2 * q:2 * q + 2, :], A_h[:, 2 * q:2 * q + 2, :].bitcast(F32),
                       ALU.subtract).then_inc(operand_ready, 2)

                def sample_heads():
                    dve.wait_ge(num_done, l * (NS * H) + (NS * H + 2))
                    for v in range(VPH):
                        TT(h_s[:, :, v, :], num_s[:, :, v, :], r_den[:, :, :], ALU.mult)
                    dve.drain()
                    TT(h_sq[:, :, :, :], h_s[:, :, :, :], h_s[:, :, :, :], ALU.mult)
                    dve.drain()
                    for v in range(1, VPH - 1):
                        TT(h_sum[:, :, :], h_sq[:, :, v, :], h_sq[:, :, 0, :] if v == 1 else h_sum[:, :, :], ALU.add)
                        dve.drain()
                    TT(h_sum[:, :, :], h_sum[:, :, :], h_sq[:, :, VPH - 1, :], ALU.add).then_inc(hs_sum_ready, 1)

                def sample_gated():
                    dve.wait_ge(hs_root, l1())
                    dve.reciprocal(h_sum[:, :, :], r_den[:, :, :])
                    dve.drain()
                    for v in range(VPH):
                        TT(h_s[:, :, v, :], h_s[:, :, v, :], h_sum[:, :, :], ALU.mult)
                    dve.drain()
                    hs_f = h_s[:, :, :, :].rearrange("p h v b -> p (h v) b")
                    TT(hs_f, hs_f, gate_s[:, :, :], ALU.mult)
                    dve.drain()
                    dve.tensor_copy(B_h[:, :, NP:T], hs_f)
                    dve.drain()
                    TT(B_l[:, :, NP:T], hs_f, B_h[:, :, NP:T].bitcast(F32), ALU.subtract).then_inc(b_ready, 1)

                dve.wait_ge(sig_done, l * 16 + 16)
                own_step(dve)
                for g in range(4):
                    for j in range(2):
                        if g < 2:
                            sample_state(28 + 2 * g + j, 2 * g + j, NS - 1, 2 * g + j)
                        ahead(l, C_PA + 2 * g + j, 2 * g + j)
                    wait_group(l, C_PA + 2 * g + 2)
                    TT(GA[:, 2 * g:2 * g + 2, :], GA[:, 2 * g:2 * g + 2, :], pair[g % 2], ALU.mult).then_inc(pair_free[g % 2], 1)
                    if g == 1:
                        sample_heads()
                    if g == 2:
                        sample_gated()

                def mix(g, idx):
                    TT(val[:, :, :], GM[:, idx, :], pair[g % 2], ALU.mult).then_inc(pair_free[g % 2], 1)
                    dve.drain()
                    TT(val[:, :, :], val[:, :, :], GA[:, idx, :], ALU.add)
                    dve.drain()
                    dve.tensor_copy(M_h[:, idx, :], val[:, :, :])
                    dve.drain()
                    TT(M_l[:, idx, :], val[:, :, :], M_h[:, idx, :].bitcast(F32), ALU.subtract).then_inc(operand_ready, 2)

                for g in range(4):
                    for j in range(4):
                        ahead(l, C_PB + 4 * g + j, j)
                    wait_group(l, C_PB + 4 * g + 4)
                    mix(g, slice(2 * g, 2 * g + 2))
                for g in range(4):
                    for j in range(2):
                        ahead(l, C_WO + 2 * g + j, 2 * g + j)
                    wait_group(l, C_WO + 2 * g + 2)
                    TT(X[:, 2 * g:2 * g + 2, :], X[:, 2 * g:2 * g + 2, :], pair[g % 2], ALU.add).then_inc(pair_free[g % 2], 1)
                    operand_los(l, g, PAR_FFN2)
                    add_squares(l, g)
                ffn(l, 1, C_FFN2, G_FFN2, 2, PARS + PAR_FFN1)

            norm_n[0] = 3
            add_squares(DEPTH, 3)
            dve.wait_ge(g_loaded, 16)
            dve.wait_ge(y_root, 1)
            dve.reciprocal(y_scale[:, 0:2], y_scale[:, 0:2])
            dve.reciprocal(y_scale[0:NS, 2:3], y_scale[0:NS, 2:3])
            dve.drain()
            for s in range(3):
                n = P if s < 2 else NS
                dve.wait_ge(y_tr, s + 1)
                for half in range(2):
                    cols = slice(half * 512, (half + 1) * 512)
                    STT(y_rows[0:n, s, cols], ps[0:n, y_banks[s] + half, :], y_scale[0:n, s:s + 1], g_rows[0:n, cols],
                        ALU.mult, ALU.mult).then_inc(y_copied, 1)

        @block.tensor
        def _(pe):
            def product(l, c, slot, n, out, src_h, src_l, k0, first, last, ready=None):
                pe.wait_ge(split_lo, l * CHUNKS + (c + (SLOTS + 1)))
                w_h = hi[slot][:, 0:n * GW].rearrange("p (k n) -> p k n", n=GW)
                w_l = lo[slot][:, 0:n * GW].rearrange("p (k n) -> p k n", n=GW)
                for f in range(2):
                    cols = slice(f * P, (f + 1) * P)
                    for k in range(n):
                        a, z = first and k == 0, last and k == n - 1
                        if ready is not None and f == 0 and k % 2 == 0:
                            operand(l, ready + k + 2)
                        pe.matmul(out[:, f, :], w_h[:, k, cols], src_h[:, k0 + k, :], start=a, stop=False)
                        pe.matmul(out[:, f, :], w_h[:, k, cols], src_l[:, k0 + k, :], start=False, stop=False)
                        ins = pe.matmul(out[:, f, :], w_l[:, k, cols], src_h[:, k0 + k, :], start=False, stop=z)
                ins.then_inc(chunk_done, 1)

            def group_free(l, g2, p):
                pe.wait_ge(pair_free[p], 1 + l * (GROUPS // 2) + g2)

            def operand(l, n):
                pe.wait_ge(operand_ready, l * OPS + n)

            def norm_sums(l, n):
                pe.wait_ge(sums_ready, l * (3 * NORMS) + 3 * (n + 1))
                pe.matmul(ps[:, 7, 0:T], ones[:, :], sq_sum[:, 0, :], start=True, stop=True).then_inc(norm_sum, 1)

            def ffn(l, which, c0, g0, op, norm):
                def pair_of(i, first):
                    for g in range(2):
                        group_free(l, i + g0 // 2, g)
                        for j in range(2):
                            product(l, i * 4 + (c0 + 2 * g + j), 2 * g + j, CK, pair[g], A_h, A_l, CK * j, j == 0, j == 1,
                                    op + CK * j if first and g == 0 else None)
                            if first and (g, j) == (0, 1):
                                norm_sums(l, norm)

                pair_of(0, True)
                with pe.Fori(1, FFN_PAIRS) as i:
                    pair_of(i, False)
                with pe.Fori(0, DOWN_GROUPS // 2) as i:
                    for g in range(2):
                        group_free(l, i + (g0 // 2 + FFN_PAIRS), g)
                        for j in range(DOWN_CHUNKS):
                            n = min(CK, FT - CK * j)
                            pe.wait_ge(hidden_ready, l * (2 * FFN_PAIRS) + (which * FFN_PAIRS + (CK * j + n) // 2))
                            s = (g * DOWN_CHUNKS + j) % SLOTS
                            product(l, i * (2 * DOWN_CHUNKS) + (c0 + C_DOWN + g * DOWN_CHUNKS + j), s, n,
                                    pair[g], G_h, G_l, CK * j, j == 0, j == DOWN_CHUNKS - 1)

            pe.wait_ge(const_ready, 1)
            pe.wait_ge(x_loaded, 16 * 3)
            for s in range(3):
                n = P if s < 2 else NS
                for k in range(KT):
                    src = x_rows[:, s, k * P:(k + 1) * P] if s < 2 else xs_rows[:, k * P:(k + 1) * P]
                    ins = pe.transpose(ps[:, (0, 2, T_BANK)[s] + k // 4, (k % 4) * n:(k % 4 + 1) * n], src, ident[0:n, 0:n])
                ins.then_inc(prep_tr, 1)
            pe.wait_ge(prep_loaded, 16 * PREP_LOADS)
            pe.transpose(ps[:, 4, 0:P], par_rows, ident[:, :])
            pe.transpose(ps[:, 4, P:P + KT], gf_rows, ident[0:KT, 0:KT]).then_inc(prep_tr, 1)
            pe.wait_ge(prep_copied, 4)
            pe.wait_ge(block1_copied, 1)
            pe.transpose(ps[0:KT, 4, 0:KT], gf_rows[:, 0:KT], ident[0:KT, 0:KT]).then_inc(num_done, 2)

            with pe.Fori(0, DEPTH) as l:
                def l1(c=0):
                    return l + (1 + c)

                ffn(l, 0, 0, 0, OP_NORM1, 0)

                def unit(c0, g0, before=lambda g, s: None, after=lambda g, s: None, end=lambda g: None, op=None):
                    for g in range(4):
                        for j in range(2):
                            before(g, j)
                            if j == 0:
                                group_free(l, g0 + g // 2, g % 2)
                            product(l, c0 + 2 * g + j, (2 * g + j) % SLOTS, CK, pair[g % 2], A_h, A_l, CK * j, j == 0, j == 1,
                                    op + CK * j if op is not None and g == 0 else None)
                            after(g, j)
                        end(g)

                unit(C_IN, G_IN // 2, op=OP_NORM2, after=lambda g, j: norm_sums(l, 1) if (g, j) == (0, 1) else None)

                pe.wait_ge(wg_ready, l1())
                for k in range(KT):
                    cols = slice(36 * k, 36 * k + P)
                    o = ps[:, T_BANK, 0:T]
                    pe.matmul(o, wg_h[:, cols], A_h[:, k, :], start=k == 0, stop=False)
                    pe.matmul(o, wg_h[:, cols], A_l[:, k, :], start=False, stop=False)
                    ins = pe.matmul(o, wg_l[:, cols], A_h[:, k, :], start=False, stop=k == KT - 1)
                ins.then_inc(gates_done, 1)

                unit(C_IN + 8, ORDER_G["k"] // 2)

                pe.wait_ge(gate_exps, l1())
                pe.wait_ge(small_loaded, l * (16 * SMALL_LOADS) + 16 * SMALL_LOADS)
                own_step(pe)
                for kind in range(3):
                    for st in range(2):
                        at = SM_AW + kind * 8 + st * 4
                        pe.transpose(ps[:, T_BANK, at:at + H], aw[:, kind, st * P:(st + 1) * P], ident[0:H, 0:H])
                for h in range(H):
                    at = SM_S + 24 * h
                    pe.matmul(ps[:, T_BANK, at:at + 24], ident[0:H, h:h + 1].broadcast_to([H, P]),
                              s_rows[:, :, :], start=True, stop=True)
                for kt in range(KPH):
                    at = SM_N + 32 * kt
                    pe.transpose(ps[:, T_BANK, at:at + 32], n_old[:, kt * P:(kt + 1) * P], ident[0:NS * H, 0:NS * H])
                for k in range(KT):
                    at = SM_CV + 16 * k
                    ins = pe.transpose(ps[:, T_BANK, at:at + 16], conv_rows[:, k * P:(k + 1) * P], ident[0:2 * NS, 0:2 * NS])
                ins.then_inc(small_done, 1)

                with pe.Fori(0, 2) as i:
                    unit(i * 8 + (C_IN + 16), i * 2 + ORDER_G["v0"] // 2)

                def tokens(t):
                    if t < 4:
                        pe.wait_ge(small_copied, l1())
                    else:
                        pe.wait_ge(tr_free[t % 2], 1 + l * 8 + t // 2)
                    for x in range(4):
                        if t < 4:
                            src = VH[:, t * 4 + x, NP:T]
                        elif t < 8:
                            src = QK[:, KT + (t // 2 - 2) * 4 + x, (t % 2) * P:(t % 2 + 1) * P]
                        else:
                            src = VH[:, (t // 2 - 4) * 4 + x, (t % 2) * P:(t % 2 + 1) * P]
                        rows_n = NS if t < 4 else P
                        ins = pe.transpose(ps[0:rows_n, token_bank(t), x * P:(x + 1) * P], src, ident[:, :])
                    ins.then_inc(tr_done, 1)

                def scores(h):
                    if h == 0:
                        for p in range(2):
                            pe.wait_ge(tr_free[p], 1 + l * 8 + 8)
                    else:
                        pe.wait_ge(cp_copied, l * (2 * H) + 2 * h)
                    for st in range(2):
                        for kt in range(KPH):
                            pe.matmul(ps[:, T_BANK, st * NP:st * NP + NP - st * P],
                                      QK[:, KT + h * KPH + kt, st * P:(st + 1) * P],
                                      QK[:, h * KPH + kt, st * P:NP], start=kt == 0, stop=kt == KPH - 1)
                    pe.matmul(ps[:, T_BANK + 1, 0:NP], ident[0:H, h:h + 1].broadcast_to([H, P]),
                              rows[:, 0, :], start=True, stop=True).then_inc(score_done, 1)

                def values(h):
                    pe.wait_ge(score_ready, l * H + (h + 1))
                    for v in range(VPH):
                        out = ps[:, T_BANK + v // 2, (v % 2) * NP:(v % 2 + 1) * NP]
                        for st in range(2):
                            w = v_tok[:, st, h * DV + v * P:h * DV + (v + 1) * P]
                            ins = pe.matmul(out[:, st * P:NP], w, score[:, st * NP:st * NP + NP - st * P],
                                            start=st == 0, stop=st == 1)
                    ins.then_inc(av_done, 1)
                    for tt in range(2):
                        for st in range(tt + 1):
                            at = st * NP + (tt - st) * P
                            pe.matmul(den_c[:, tt, h:h + 1], score[:, at:at + P], ones[:, 0:1], start=st == 0, stop=st == tt)

                def head_columns(h):
                    pe.wait_ge(av_read, l * H + (h + 1))
                    for tt in range(2):
                        for v in range(VPH):
                            at = (v % 2) * NP + tt * P
                            ins = pe.matmul(ms_c[:, tt, h:h + 1], stage[:, v // 2, at:at + P], ones[:, 0:1],
                                            start=v == 0, stop=v == VPH - 1)
                    ins.then_inc(columns_done, 1)

                def prompt_state(h):
                    for n in range(KPH * h, KPH * h + KPH):
                        for st in range(2):
                            ins = pe.matmul(np_ps[:, n:n + 1], k_tok[:, st, n * P:(n + 1) * P], ones[:, 0:1], start=st == 0, stop=st == 1)
                    ins.then_inc(np_done, 1)
                    for n in range(KPH * h, KPH * h + KPH):
                        for st in range(2):
                            ins = pe.matmul(ps[:, T_BANK + n % 2, :], k_tok[:, st, n * P:(n + 1) * P],
                                            v_tok[:, st, h * DV:(h + 1) * DV], start=st == 0, stop=st == 1)
                        ins.then_inc(cp_done, 1)

                def broadcast_v(n, b, h):
                    pe.wait_ge(c_new, 1 + l * (NS * H) + n)
                    pe.matmul(ps[:, V_BANK, :], pick[:, b:b + 1].broadcast_to([P, P]),
                              v_rows[:, bass.ds(h * DV, DV)], start=True, stop=True).then_inc(vbc_done, 1)

                def numerator(n, s, b, h, added=False):
                    pe.wait_ge(c_new, 1 + l * (NS * H) + (n + 1))
                    if added:
                        pe.wait_ge(q_c_ready, l * SUMMED + (n + 1))
                        for v in range(VPH):
                            out = num_s[:, bass.ds(h, 1), v, b:b + 1].rearrange("p a c -> p (a c)")
                            ins = pe.matmul(out, q_c[:, v * P:(v + 1) * P], ones[:, 0:1], start=True, stop=True)
                        ins.then_inc(num_done, 1)
                        return
                    for v in range(VPH):
                        for kt in range(KPH):
                            out = num_s[:, bass.ds(h, 1), v, b:b + 1].rearrange("p a c -> p (a c)")
                            q = q_s[:, bass.ds(h, 1), kt, b:b + 1].rearrange("p a c -> p (a c)")
                            ins = pe.matmul(out, C[s][:, kt, v * P:(v + 1) * P], q, start=kt == 0, stop=kt == KPH - 1)
                    ins.then_inc(num_done, 1)

                def sample_den():
                    pe.wait_ge(qn_ready, l1())
                    pe.matmul(den_s, ones[:, :], qn_sum[:, :, :], start=True, stop=True)
                    for kt in range(KPH):
                        ins = pe.transpose(n_rows_ps[:, kt * P:(kt + 1) * P], n_new[:, kt, :, :].rearrange("p h b -> p (h b)"), ident[:, :])
                    ins.then_inc(den_done, 1)

                def samples(i, n0):
                    h = i + (n0 - 12) // 4
                    return (lambda g, j: None if j else broadcast_v(i * 4 + (n0 + g), g, h),
                            lambda g, j: numerator(i * 4 + (n0 + g), 2 + g, g, h) if j and not state_chunk(i, g, n0) else None)

                def l1_before(i, j):
                    if (i, j) == (1, 0):
                        for p in range(2):
                            pe.wait_ge(tr_free[p], 1 + l * 8 + 2)
                        sample_den()
                    for n in l1_states(i, j):
                        broadcast_v(n, 4 + n // H, n % H)

                def l1_after(i, j):
                    if (i, j) == (1, 1):
                        pe.wait_ge(n_out_ready, l1())
                    for n in l1_states(i, 0) if j else ():
                        numerator(n, n % 2, 4 + n // H, n % H, n < SUMMED)
                    for n in l1_states(i, 1) if j else ():
                        numerator(n, n % 2, 4 + n // H, n % H)
                    if i >= 5 and i % 2 == 1 and j == 0:
                        head_columns((i - 5) // 2)
                        prompt_state((i - 5) // 2)

                def l1_end(i):
                    if i == 0:
                        for p in range(2):
                            pe.wait_ge(pair_free[p], 1 + l * (GROUPS // 2) + ORDER_G["gc"] // 2)
                    if i < 4:
                        for t in range(4 * i, 4 * i + 4):
                            tokens(t)
                    if i >= 3 and i % 2 == 1 and i < 11:
                        scores((i - 3) // 2)
                    if i >= 4 and i % 2 == 0:
                        values((i - 4) // 2)

                unit(C_IN + 32, ORDER_G["gc"] // 2, l1_before, l1_after, l1_end)
                unit(C_IN + 40, ORDER_G["xa"] // 2, lambda g, j: l1_before(4 + g, j), lambda g, j: l1_after(4 + g, j),
                     lambda g: l1_end(4 + g))
                unit(C_IN + 48, ORDER_G["gb"] // 2, lambda g, j: l1_before(8 + g, j), lambda g, j: l1_after(8 + g, j),
                     lambda g: l1_end(8 + g))

                pe.wait_ge(cp_copied, l * (2 * H) + 2 * H)
                for k in range(KT):
                    ins = pe.transpose(ps[0:2 + NS, T_BANK + k // 4, (k % 4) * P:(k % 4 + 1) * P], u_keep[:, k, :], ident[:, :])
                ins.then_inc(tail_done, 1)

                def factors():
                    pe.wait_ge(columns_read, l1())
                    pe.transpose(npt_ps, np_col[:, :], ident[:, :]).then_inc(npt_done, 1)
                    pe.wait_ge(tail_copied, l1())
                    for half in range(2):
                        pe.wait_ge(diag_ready, l * 2 + (half + 1))
                        for x in range(4):
                            ins = pe.matmul(ps[:, T_BANK + half, x * P:(x + 1) * P], ones[:, :], diag[half][:, x, :], start=True, stop=True)
                        ins.then_inc(factors_done, 1)

                for i in range(2):
                    unit(i * 8 + (C_IN + 56), i * 2 + ORDER_G["o0"] // 2, *samples(i, 12),
                         lambda g: (numerator(12, 2, 0, 0), factors()) if (i, g) == (0, 0) else None)
                with pe.Fori(0, 2) as i:
                    unit(i * 8 + (C_IN + 72), i * 2 + ORDER_G["ga"] // 2, *samples(i, 20))

                for g in range(4):
                    group_free(l, (G_PA + g) // 2, g % 2)
                    for j in range(2):
                        h = 2 * g + j
                        if h < H:
                            broadcast_v(28 + h, NS - 1, h)
                        product(l, C_PA + 2 * g + j, (2 * g + j) % SLOTS, CK, pair[g % 2], A_h, A_l, CK * j, j == 0, j == 1,
                                OP_YA + CK * j if g == 0 else None)
                        if h < H:
                            numerator(28 + h, h, NS - 1, h)
                    if g == 2:
                        pe.wait_ge(hs_sum_ready, l1())
                        own_step(pe)
                        pe.matmul(den_s, ones[:, :], h_sum[:, :, :], start=True, stop=True).then_inc(hs_sum, 1)
                pe.wait_ge(b_ready, 1 + l * 9 + 9)
                own_step(pe)
                with pe.Fori(0, 2) as i:
                    for g in range(2):
                        group_free(l, i + G_PB // 2, g)
                        for j in range(4):
                            product(l, i * 8 + (C_PB + 4 * g + j), j, CK, pair[g], B_h, B_l, CK * j, j == 0, j == 3)
                with pe.Fori(0, 2) as i:
                    for g in range(2):
                        group_free(l, i + G_WO // 2, g)
                        for j in range(2):
                            product(l, i * 4 + (C_WO + 2 * g + j), 2 * g + j, CK, pair[g], M_h, M_l, CK * j, j == 0, j == 1,
                                    OP_MIX + CK * j)
                ffn(l, 1, C_FFN2, G_FFN2, OP_NORM3, 2)

            def y_transposes(s, tiles):
                n = P if s < 2 else NS
                for k in tiles:
                    ins = pe.transpose(ps[0:n, y_banks[s] + k // 4, (k % 4) * P:(k % 4 + 1) * P], X[:, k, s * P:s * P + n], ident[:, :])
                return ins

            pe.wait_ge(pair_free[0], 1 + DEPTH * (GROUPS // 2))
            pe.wait_ge(x_ready, 1 + DEPTH * 8 - 1)
            for s in range(2):
                y_transposes(s, range(KT - 2))
            pe.wait_ge(sums_ready, DEPTH * (3 * NORMS) + 3)
            for s in range(3):
                n = P if s < 2 else NS
                ins = pe.matmul(y_rms[0:n, s:s + 1], sq_sum[:, 0, s * P:s * P + n], ones[:, 0:1], start=True, stop=True)
            ins.then_inc(y_sums, 1)
            for s in range(3):
                y_transposes(s, range(KT - 2, KT) if s < 2 else range(KT)).then_inc(y_tr, 1)


INPUTS = ["x_prompt", "x_sample", "state_conv", "state_mlstm_c", "state_mlstm_n", "state_mlstm_m",
          "g_ffn1", "w_ffn1_gu", "w_ffn1_down", "g_mix", "w_in", "w_conv", "b_igate", "b_fgate", "g_head",
          "w_proj_a", "w_proj_b", "w_out", "g_ffn2", "w_ffn2_gu", "w_ffn2_down", "g_final"]
OUTPUTS = [(1, NP, D), (NS, 1, D), (DEPTH, 1, 2, D), (DEPTH, 1, H, DK, DV), (DEPTH, 1, H, DK), (DEPTH, 1, H),
           (DEPTH, NS, 2, D), (DEPTH, NS, H, DK, DV), (DEPTH, NS, H, DK), (DEPTH, NS, H)]


def kernel(**inputs):
    import numpy as np
    import concourse.bacc as bacc
    from concourse.bass_utils import run_bass_kernel_spmd as run

    nc = bacc.Bacc("TRN2", target_bir_lowering=False, num_devices=1, dynamic_dma_scratch_size=SCRATCH)
    arrays, args = {}, []
    for name in INPUTS:
        a = np.ascontiguousarray(inputs[name])
        arrays[f"in_{name}"] = a
        args.append(nc.dram_tensor(f"in_{name}", a.shape, mybir.dt.from_np(a.dtype), kind="ExternalInput").ap())
    for i, shape in enumerate(OUTPUTS):
        args.append(nc.dram_tensor(f"out_{i}", shape, F32, kind="ExternalOutput").ap())
    build_program(nc, *args)
    r = run(nc, [arrays], core_ids=[0])
    return tuple(r.results[0][f"out_{i}"] for i in range(len(OUTPUTS)))
```
